# Optimizing a Trainium2 kernel written in Bass

```python
import jax, jax.numpy as jnp
from jax import lax
import numpy as np

D_MODEL = 1024
BATCH = 1
SEQ = 512
DEPTH = 1

HEAD_DIM = 64
A_HEADS = 6
B_HEADS = 6
C_HEADS = 4
A_WIDTH = A_HEADS * HEAD_DIM
B_WIDTH = B_HEADS * HEAD_DIM
C_WIDTH = C_HEADS * HEAD_DIM
MIX_WIDTH = A_WIDTH + B_WIDTH + C_WIDTH
DECAY_LORA = 64
AAA_LORA = 64
GATE_LORA = 128
VRES_LORA = 32
A_COLS = 3 * A_WIDTH + DECAY_LORA + AAA_LORA + GATE_LORA
B_COLS = 3 * B_WIDTH + B_HEADS
C_COLS = 3 * C_WIDTH
IN_COLS = A_COLS + B_COLS + C_COLS
A_SPLITS = (A_WIDTH, 2 * A_WIDTH, 3 * A_WIDTH, 3 * A_WIDTH + DECAY_LORA, 3 * A_WIDTH + DECAY_LORA + AAA_LORA)
B_SPLITS = (B_WIDTH, 2 * B_WIDTH, 3 * B_WIDTH)
C_SPLITS = (C_WIDTH, 2 * C_WIDTH)
MEM_LEN = 256
MEM_HEADS = 4
MEM_HEAD_DIM = D_MODEL // MEM_HEADS
D_FF = -(-(8 * D_MODEL) // (3 * 256)) * 256
Q_BLOCK = 128
RMS_EPS = 1e-6
GN_EPS = 64e-5
ATTN_SCALE = HEAD_DIM ** -0.5
MEM_SCALE = MEM_HEAD_DIM ** -0.5

kernel_name = "hybrid_rwkv7_fox_stickbreak_block"

def _rmsnorm(x, g):
    xf = x.astype(jnp.float32)
    y = xf * lax.rsqrt(jnp.mean(xf * xf, axis=-1, keepdims=True) + RMS_EPS)
    return (y * g.astype(jnp.float32)).astype(x.dtype)

def _split_heads(z, n_heads):
    b, t, _ = z.shape
    return z.reshape(b, t, n_heads, -1).transpose(0, 2, 1, 3)

def _merge_heads(z):
    b, h, t, d = z.shape
    return z.transpose(0, 2, 1, 3).reshape(b, t, h * d)

def _query_blocks(z):
    b, h, t = z.shape[:3]
    z = z.reshape((b, h, t // Q_BLOCK, Q_BLOCK) + z.shape[3:])
    return jnp.moveaxis(z, 2, 0)

def _unblock(o):
    nb, b, h, q, d = o.shape
    return jnp.moveaxis(o, 0, 2).reshape(b, h, nb * q, d)

def _rwkv7_scan(r, w, k, v, a, b):
    bsz, t, h, n = r.shape
    seq_first = lambda u: jnp.moveaxis(u.astype(jnp.float32), 1, 0)

    def step(S, inp):
        r_t, w_t, k_t, v_t, a_t, b_t = inp
        Sa = jnp.einsum('bhij,bhj->bhi', S, a_t)
        S = S * w_t[:, :, None, :] + Sa[..., None] * b_t[:, :, None, :] + v_t[..., None] * k_t[:, :, None, :]
        return S, jnp.einsum('bhij,bhj->bhi', S, r_t)

    S0 = jnp.zeros((bsz, h, n, n), jnp.float32)
    _, y = lax.scan(step, S0, (seq_first(r), seq_first(w), seq_first(k), seq_first(v), seq_first(a), seq_first(b)))
    return jnp.moveaxis(y, 0, 1)

def _rwkv7_mixer(z, mu, w0, w_up, a0, a_up, g_up, k_k, k_a, r_k, gn_g, gn_b, v_first, vres):
    z_prev = jnp.pad(z[:, :-1], ((0, 0), (1, 0), (0, 0)))
    z = z + (z_prev - z) * mu
    r, k, v, wd, ad, gd = jnp.split(z, A_SPLITS, axis=-1)
    w_log = -jax.nn.softplus(-(w0 + jnp.tanh(wd) @ w_up)) - 0.5
    decay = jnp.exp(-jnp.exp(w_log.astype(jnp.float32)))
    a = jax.nn.sigmoid(a0 + ad @ a_up)
    g = jax.nn.sigmoid(gd) @ g_up
    if vres is None:
        v_first = v
    else:
        v_bias, v_down, v_up = vres
        v = v + (v_first - v) * jax.nn.sigmoid(v_bias + (v @ v_down) @ v_up)
    bsz, t, _ = z.shape
    hs = lambda u: u.reshape(bsz, t, A_HEADS, HEAD_DIM)
    kk = hs(k * k_k).astype(jnp.float32)
    kk = kk * lax.rsqrt(jnp.maximum(jnp.sum(kk * kk, axis=-1, keepdims=True), 1e-24))
    k = k * (1.0 + (a - 1.0) * k_a)
    r4, k4, v4, a4 = hs(r), hs(k), hs(v), hs(a)
    y = _rwkv7_scan(r4, hs(decay), k4, v4, -kk, kk * a4.astype(jnp.float32))
    mean = jnp.mean(y, axis=-1, keepdims=True)
    var = jnp.mean(jnp.square(y - mean), axis=-1, keepdims=True)
    y = ((y - mean) * lax.rsqrt(var + GN_EPS)).reshape(bsz, t, A_WIDTH) * gn_g + gn_b
    bonus = (jnp.sum(r4 * k4 * r_k, axis=-1, keepdims=True) * v4).reshape(bsz, t, A_WIDTH)
    return (y.astype(z.dtype) + bonus) * g, v_first

def _fox_mixer(z, f_bias):
    q, k, v, fl = jnp.split(z, B_SPLITS, axis=-1)
    logf = jax.nn.log_sigmoid((fl + f_bias).astype(jnp.float32))
    c = jnp.cumsum(logf, axis=1).transpose(0, 2, 1)
    q, k, v = (_split_heads(u, B_HEADS) for u in (q, k, v))
    t = q.shape[2]
    k_pos = jnp.arange(t)

    def block(args):
        q_blk, c_blk, blk = args
        s = jnp.einsum('bhqd,bhkd->bhqk', q_blk, k).astype(jnp.float32) * ATTN_SCALE
        s = s + c_blk[..., None] - c[:, :, None, :]
        q_pos = blk * Q_BLOCK + jnp.arange(Q_BLOCK)
        s = jnp.where(k_pos[None, :] <= q_pos[:, None], s, -jnp.inf)
        p = jax.nn.softmax(s, axis=-1)
        return jnp.einsum('bhqk,bhkd->bhqd', p.astype(v.dtype), v)

    o = lax.map(block, (_query_blocks(q), _query_blocks(c), jnp.arange(t // Q_BLOCK)))
    return _merge_heads(_unblock(o))

def _stick_breaking_mixer(z):
    q, k, v = jnp.split(z, C_SPLITS, axis=-1)
    q, k, v = (_split_heads(u, C_HEADS) for u in (q, k, v))
    t = q.shape[2]
    k_pos = jnp.arange(t)

    def block(args):
        q_blk, blk = args
        logits = jnp.einsum('bhqd,bhkd->bhqk', q_blk, k).astype(jnp.float32) * ATTN_SCALE
        q_pos = blk * Q_BLOCK + jnp.arange(Q_BLOCK)
        mask = k_pos[None, :] < q_pos[:, None]
        log_rest = jnp.where(mask, jax.nn.log_sigmoid(-logits), 0.0)
        later = lax.cumsum(log_rest, axis=3, reverse=True) - log_rest
        att = jnp.where(mask, jnp.exp(jax.nn.log_sigmoid(logits) + later), 0.0)
        return jnp.einsum('bhqk,bhkd->bhqd', att.astype(v.dtype), v)

    o = lax.map(block, (_query_blocks(q), jnp.arange(t // Q_BLOCK)))
    return _merge_heads(_unblock(o))

def _memory_attention(h, mem_n, wq, wkv, wo):
    q = _split_heads(h @ wq, MEM_HEADS)
    mk, mv = jnp.split(mem_n @ wkv, 2, axis=-1)
    mk, mv = _split_heads(mk, MEM_HEADS), _split_heads(mv, MEM_HEADS)
    s = jnp.einsum('bhqd,bhkd->bhqk', q, mk).astype(jnp.float32) * MEM_SCALE
    p = jax.nn.softmax(s, axis=-1)
    o = jnp.einsum('bhqk,bhkd->bhqd', p.astype(mv.dtype), mv)
    return _merge_heads(o) @ wo

def setup_inputs(seed: int = 0) -> dict:
    key = jax.random.key(seed)
    keys = iter(jax.random.split(key, 48))
    nrm = lambda shape, scale: jax.random.normal(next(keys), shape, jnp.float32) * scale
    uni = lambda shape, lo, hi: jax.random.uniform(next(keys), shape, jnp.float32, lo, hi)
    gain = lambda shape: 1.0 + nrm(shape, 0.02)
    L, D = DEPTH, D_MODEL
    return {
        "x": nrm((BATCH, SEQ, D), 1.0),
        "mem": nrm((BATCH, MEM_LEN, D), 1.0),
        "norm_mix_pre": gain((L, D)),
        "norm_mix_post": gain((L, D)),
        "w_in": nrm((L, D, IN_COLS), D ** -0.5),
        "shift_mu": uni((L, A_COLS), 0.0, 1.0),
        "rwkv_w0": uni((L, A_WIDTH), -6.5, -1.0),
        "rwkv_w_up": nrm((L, DECAY_LORA, A_WIDTH), 0.1 * DECAY_LORA ** -0.5),
        "rwkv_a0": nrm((L, A_WIDTH), 0.1),
        "rwkv_a_up": nrm((L, AAA_LORA, A_WIDTH), 0.5 * AAA_LORA ** -0.5),
        "rwkv_g_up": nrm((L, GATE_LORA, A_WIDTH), GATE_LORA ** -0.5),
        "rwkv_k_k": 0.85 + nrm((L, A_WIDTH), 0.02),
        "rwkv_k_a": gain((L, A_WIDTH)),
        "rwkv_r_k": -0.04 + nrm((L, A_HEADS, HEAD_DIM), 0.02),
        "rwkv_gn_g": gain((L, A_WIDTH)),
        "rwkv_gn_b": nrm((L, A_WIDTH), 0.02),
        "vres_bias": 1.0 + nrm((L - 1, A_WIDTH), 0.1),
        "vres_down": nrm((L - 1, A_WIDTH, VRES_LORA), A_WIDTH ** -0.5),
        "vres_up": nrm((L - 1, VRES_LORA, A_WIDTH), 0.5 * VRES_LORA ** -0.5),
        "fox_f_bias": uni((L, B_HEADS), 1.0, 4.0),
        "w_out": nrm((L, MIX_WIDTH, D), MIX_WIDTH ** -0.5),
        "norm_mem_pre": gain((L, D)),
        "norm_mem_post": gain((L, D)),
        "norm_mem_kv": gain((L, D)),
        "mem_wq": nrm((L, D, D), D ** -0.5),
        "mem_wkv": nrm((L, D, 2 * D), D ** -0.5),
        "mem_wo": nrm((L, D, D), D ** -0.5),
        "norm_ffn_pre": gain((L, D)),
        "norm_ffn_post": gain((L, D)),
        "ffn_w_gu": nrm((L, D, 2 * D_FF), D ** -0.5),
        "ffn_w_down": nrm((L, D_FF, D), D_FF ** -0.5),
    }

def reference(x, mem, norm_mix_pre, norm_mix_post, w_in, shift_mu, rwkv_w0, rwkv_w_up, rwkv_a0, rwkv_a_up,
              rwkv_g_up, rwkv_k_k, rwkv_k_a, rwkv_r_k, rwkv_gn_g, rwkv_gn_b, vres_bias, vres_down, vres_up,
              fox_f_bias, w_out, norm_mem_pre, norm_mem_post, norm_mem_kv, mem_wq, mem_wkv, mem_wo,
              norm_ffn_pre, norm_ffn_post, ffn_w_gu, ffn_w_down):
    v_first = None
    for l in range(DEPTH):
        h = _rmsnorm(x, norm_mix_pre[l])
        z_a, z_b, z_c = jnp.split(h @ w_in[l], (A_COLS, A_COLS + B_COLS), axis=-1)
        vres = None if l == 0 else (vres_bias[l - 1], vres_down[l - 1], vres_up[l - 1])
        y_a, v_first = _rwkv7_mixer(z_a, shift_mu[l], rwkv_w0[l], rwkv_w_up[l], rwkv_a0[l], rwkv_a_up[l],
                                    rwkv_g_up[l], rwkv_k_k[l], rwkv_k_a[l], rwkv_r_k[l], rwkv_gn_g[l],
                                    rwkv_gn_b[l], v_first, vres)
        y_b = _fox_mixer(z_b, fox_f_bias[l])
        y_c = _stick_breaking_mixer(z_c)
        mixed = jnp.concatenate([y_a, y_b, y_c], axis=-1) @ w_out[l]
        x = x + _rmsnorm(mixed, norm_mix_post[l])
        h = _rmsnorm(x, norm_mem_pre[l])
        mem_n = _rmsnorm(mem, norm_mem_kv[l])
        x = x + _rmsnorm(_memory_attention(h, mem_n, mem_wq[l], mem_wkv[l], mem_wo[l]), norm_mem_post[l])
        h = _rmsnorm(x, norm_ffn_pre[l])
        gate, up = jnp.split(h @ ffn_w_gu[l], 2, axis=-1)
        x = x + _rmsnorm((jax.nn.silu(gate) * up) @ ffn_w_down[l], norm_ffn_post[l])
    return x


_drawn_inputs = setup_inputs


def setup_inputs(seed=0):
    import zlib

    import numpy as np

    out = dict(_drawn_inputs(seed))
    spreads = {}
    factors = {'norm_mix_post': 3.787,
     'rwkv_w_up': 8.0,
     'rwkv_a0': 2.869,
     'rwkv_k_k': 5.361,
     'rwkv_k_a': 5.352,
     'rwkv_gn_g': 5.807,
     'rwkv_gn_b': 5.071,
     'norm_mem_pre': 4.252,
     'norm_mem_post': 13.547,
     'norm_mem_kv': 3.054,
     'norm_ffn_pre': 13.961,
     'norm_ffn_post': 22.004}
    for name, (base, spread) in spreads.items():
        noise = np.random.default_rng([zlib.crc32(name.encode()), seed]).standard_normal(out[name].shape)
        drawn = base * np.exp(spread * noise) if base else spread * noise
        out[name] = __import__('jax').numpy.asarray(drawn.astype(out[name].dtype))
    for name, factor in factors.items():
        out[name] = (out[name] * factor).astype(out[name].dtype)
    return out
```

```python
import numpy as np
import concourse.bass as bass
from concourse import mybir
from contextlib import ExitStack

F32 = mybir.dt.float32
F32R = mybir.dt.float32r
BF16 = mybir.dt.bfloat16
ALU = mybir.AluOpType
ACT = mybir.ActivationFunctionType
AX = mybir.AxisListType

P = 128
D = 1024
T = 512
NT = T // P
KT = D // P
HD = 64
AH, BH, CH = 6, 6, 4
AW, BW, CW = AH * HD, BH * HD, CH * HD
APAIRS = AH // 2
LORA = 64
A_COLS = 3 * AW + 2 * LORA + 128
B_COLS = 3 * BW + BH
A_TILES = A_COLS // P
Q_TILES = (2 * BW + 2 * CW) // P
VB_W, VC_W = BW + BH, CW
ML = 256
MT = ML // P
MH, MHD = 4, 256
FF = 2816
FT = FF // P
CHUNK = 64
LEVELS = [2, 4, 8, 16, 32]
RMS_EPS = 1e-6
GN_EPS = 64e-5
DECAY_C = float(np.exp(-0.5))
BIG = 1e30

P_A = 0
P_Q = P_A + A_TILES
P_VB = P_Q + Q_TILES
P_VC = P_VB + KT // 2
P_WO = P_VC + KT // 2
P_MK = P_WO + KT
P_MV = P_MK + KT
P_MQ = P_MV + KT
P_MO = P_MQ + KT
P_GU = P_MO + KT
P_DN = P_GU + 2 * FT
P_END = P_DN + FT

V_MU = 0
V_W0, V_A0, V_KK, V_KA, V_RK, V_GG, V_GB = (A_TILES + APAIRS * n for n in range(7))
V_ROWS = A_TILES + 7 * APAIRS
SMALL_LOADS = 16 * 12
RW_STEPS = 12


def panel_run(eng, first, count, unroll, body):
    peeled = 2 if first == 0 else 0
    for j in range(peeled):
        body(j, first + j, (first + j) % 2, (first + j) // 2)
    turns = (count - peeled) // unroll
    done = peeled
    if turns > 1:
        with eng.Fori(0, turns) as turn:
            for s in range(unroll):
                p = first + peeled + s
                body(peeled + s + unroll * turn, p + unroll * turn, p % 2, p // 2 + (unroll // 2) * turn)
        done += turns * unroll
    for j in range(done, count):
        body(j, first + j, (first + j) % 2, (first + j) // 2)


def hybrid_block(nc, x, mem, norm_mix_pre, norm_mix_post, w_in, shift_mu, rwkv_w0, rwkv_w_up, rwkv_a0, rwkv_a_up,
                 rwkv_g_up, rwkv_k_k, rwkv_k_a, rwkv_r_k, rwkv_gn_g, rwkv_gn_b, fox_f_bias, w_out, norm_mem_pre,
                 norm_mem_post, norm_mem_kv, mem_wq, mem_wkv, mem_wo, norm_ffn_pre, norm_ffn_post, ffn_w_gu,
                 ffn_w_down, out):
    ctx = ExitStack()
    with ctx:
        def sb(name, shape, dt=F32, where=ctx):
            return where.enter_context(nc.sbuf_tensor(name, shape, dt))

        sems = {}

        def sig(name):
            if name not in sems:
                sems[name] = ctx.enter_context(nc.semaphore(name))
            return sems[name]

        xt = sb("xt", [P, NT, D])
        act_hi = sb("act_hi", [P, KT, T], F32R)
        act_lo = sb("act_lo", [P, KT, T], F32R)
        raw = [sb(f"raw{s}", [P, D]) for s in range(2)]
        w_hi = [sb(f"w_hi{s}", [P, D], F32R) for s in range(2)]
        w_lo = [sb(f"w_lo{s}", [P, D], F32R) for s in range(2)]
        gain = [sb(f"gain{b}", [P, D]) for b in range(2)]
        ident = sb("ident", [P, P])
        pair_ones = sb("pair_ones", [P, P])
        vec_rows = sb("vec_rows", [V_ROWS, P])
        vecs = sb("vecs", [P, V_ROWS])
        ssq = sb("ssq", [P, 8])
        var = sb("var", [P, 8])
        std = sb("std", [P, 8])
        rstd = sb("rstd", [P, 8])
        scrap1 = sb("scrap1", [P, 1])

        mix = ExitStack()
        z = sb("z", [P, A_TILES, T], where=mix)
        sigw = sb("sigw", [P, APAIRS, T], where=mix)
        clog = sb("clog", [P, APAIRS, T], where=mix)
        nkk = sb("nkk", [P, APAIRS, T], where=mix)
        kka = sb("kka", [P, APAIRS, T], where=mix)
        gate = sb("gate", [P, APAIRS, T], where=mix)
        lora_w = sb("lora_w", [P, AW], where=mix)
        gate_w = sb("gate_w", [P, AW], where=mix)
        omka = sb("omka", [P, APAIRS], where=mix)
        reset = sb("reset", [P, T], where=mix)
        grams = sb("gram_mask", [P, 2 * P], where=mix)
        lowm = sb("lowm", [P, P], where=mix)
        lowmT = sb("lowmT", [P, P], where=mix)
        levm = sb("levm", [P, len(LEVELS), P], where=mix)
        stack_id = sb("stack_id", [P, HD], where=mix)
        att = ExitStack()
        qk = sb("qk", [P, Q_TILES, T], where=att)
        vB = sb("vB", [P, NT, VB_W], where=att)
        vC = sb("vC", [P, NT, VC_W], where=att)
        tri_ones = sb("tri_ones", [P, T], where=att)
        ntri = sb("ntri", [P, P], where=att)
        nones = sb("nones", [P, P], where=att)
        ident_b = sb("ident_b", [P, P], BF16, where=att)
        fmask_b = sb("fmask_b", [P, P], BF16, where=att)
        smask_b = sb("smask_b", [P, P], BF16, where=att)
        smask = sb("smask", [P, P], where=att)
        lf = sb("lf", [P, NT, BH], where=att)
        lf2 = sb("lf2", [P, NT, BH], where=att)
        fbias = sb("fbias", [P, BH], where=att)
        small_t = sb("small_t", [P, 4, 4], where=att)
        wk_base = ExitStack()
        hn = sb("hn", [P, 2, D], where=wk_base)
        zraw = sb("zraw", [P, 2, T + 8], where=wk_base)
        junk = sb("junk", [P, D], where=wk_base)
        zs = sb("zs", [P, APAIRS, T], where=wk_base)
        wk_base.close()
        fox_ctx = ExitStack()
        cb = sb("cb", [P, 2, T], where=fox_ctx)
        fs = sb("fs", [P, 3, T], where=fox_ctx)
        fp = sb("fp", [P, 3, T], where=fox_ctx)
        fpt = sb("fpt", [P, 2, T], where=fox_ctx)
        fox_ctx.close()
        stick_ctx = ExitStack()
        NJ = [T - P * j for j in range(NT)]
        OJ = [sum(NJ[:j]) for j in range(NT)]
        SB_W = sum(NJ)
        sp = sb("sp", [P, 2, SB_W], where=stick_ctx)
        satt = sb("satt", [P, 2, SB_W], where=stick_ctx)
        se = sb("se", [P, 2, T], where=stick_ctx)
        stick_ctx.close()
        att.close()
        rw = ExitStack()
        E = sb("E", [P, 3, APAIRS, P], where=rw)
        lp = sb("lp", [P, APAIRS, P], where=rw)
        Vt = sb("Vt", [P, APAIRS, P], where=rw)
        Dg = sb("Dg", [P, 2, APAIRS, HD], where=rw)
        AR = sb("AR", [P, APAIRS, 2, P], where=rw)
        BK = sb("BK", [P, 2, APAIRS, P], where=rw)
        BKh = sb("BKh", [P, 2, APAIRS, P], where=rw)
        tokBK = sb("tokBK", [P, 2, AH, HD], where=rw)
        tokV = sb("tokV", [P, AH, HD], where=rw)
        G1 = sb("G1", [P, AH, 2 * P], where=rw)
        G2 = sb("G2", [P, AH, 2 * P], where=rw)
        Tm = sb("Tm", [P, AH, P], where=rw)
        TT = sb("TT", [P, AH, P], where=rw)
        X = sb("X", [P, AH, P], where=rw)
        RHS = sb("RHS", [P, AH, P], where=rw)
        WU = Tm
        GT = sb("GT", [P, APAIRS, P], where=rw)
        PT = sb("PT", [P, 2, APAIRS, P], where=rw)
        QS = sb("QS", [P, 2, APAIRS, HD], where=rw)
        St = sb("St", [P, 3, APAIRS, HD], where=rw)
        Sbd = sb("Sbd", [P, 2, APAIRS, P], where=rw)
        Y = sb("Y", [P, APAIRS, T], where=rw)
        rw.close()
        fin_ctx = ExitStack()
        yq = sb("yq", [P, APAIRS, 4, T], where=fin_ctx)
        fin_ctx.close()
        mix.close()

        ma = ExitStack()
        ybuf = sb("ybuf", [P, NT, D], where=ma)
        hn2 = sb("hn2", [P, 2, D], where=ma)
        junk2 = sb("junk2", [P, D], where=ma)
        ff = ExitStack()
        a_hi = sb("a_hi", [P, FT, T], F32R, where=ff)
        a_lo = sb("a_lo", [P, FT, T], F32R, where=ff)
        ftmp = sb("ftmp", [P, 4, T], where=ff)
        junk_f = sb("junk_f", [P, T], where=ff)
        ff.close()

        mx = sb("mx", [P, MT, D], where=ma)
        mem_hi = sb("mem_hi", [P, KT, ML], F32R, where=ma)
        mem_lo = sb("mem_lo", [P, KT, ML], F32R, where=ma)
        mk = sb("mk", [P, KT, ML], where=ma)
        mv = sb("mv", [P, MT, D], where=ma)
        mq = sb("mq", [P, KT, T], where=ma)
        mp = sb("mp", [P, 2, ML], where=ma)
        mpt = sb("mpt", [P, 2, MT, T], where=ma)
        msm = sb("msm", [P, 4, 4], where=ma)
        ssq2 = sb("ssq2", [P, 8], where=ma)
        ma.close()

        ps = [ctx.enter_context(nc.psum_tensor(f"ps{b}", [P, T], F32)) for b in range(8)]

        def fm_cols(w, at):
            return w[0].rearrange("(k p) n -> p k n", p=P)[:, :, bass.ds(at, P)]

        def tm_rows(w, pair, at, width):
            return w[0].rearrange("(k p) n -> p k n", p=P)[:, 2 * pair:2 * pair + 2, at:at + width]

        def q_col(j):
            return A_COLS + P * j if j < 2 * BW // P else A_COLS + B_COLS + P * (j - 2 * BW // P)

        class Steps:
            def __init__(self, eng, sem, base=0):
                self.eng, self.sem, self.base, self.n = eng, sem, base, 0

            def step(self, ins):
                ins.then_inc(self.sem, 1)
                self.n += 1
                return self.n

            def sync(self, n=None):
                self.eng.wait_ge(self.sem, self.base + (self.n if n is None else n))

        GAINS = [norm_mix_pre, norm_mem_kv, norm_mix_post, norm_mem_pre, norm_mem_post, norm_ffn_pre, norm_ffn_post]

        def gain_load(eng, g):
            eng.dma_start(gain[g % 2][:, :], GAINS[g][0].partition_broadcast(P)).then_inc(sig(f"gain_loaded{g % 2}"), 16)

        def gain_wait(eng, g):
            eng.wait_ge(sig(f"gain_loaded{g % 2}"), 16 * (g // 2 + 1))

        EACH = {"pre_sq": 1, "pre_hn": 1, "pre_tr": 2, "pre_hi": 2, "pre_lo": 2, "post_sq": 2, "post_out": 2,
                "x_new": 1, "pre_var": 1, "pre_std": 1, "pre_rstd": 1}
        ONCE = {"post_var": 2, "post_std": 1, "post_rstd": 1}

        def stage(name, s, n):
            order = [0, "m", 1, 2] if name.startswith("pre") else [1, 2, 3]
            before = order[:order.index(s)]
            tiles = sum(MT if b == "m" else NT for b in before)
            return sig(name), n + (EACH[name] * tiles if name in EACH else ONCE[name] * len(before))

        def pre_act(act, s, src, scrap, tile_ready, dst_hi, banks):
            def square(t):
                act.wait_ge(*tile_ready(t))
                if t:
                    act.wait_ge(*stage("pre_sq", s, t))
                act.activation(scrap, src[:, t, :], ACT.Square, accum_out=ssq[:, t:t + 1]).then_inc(sig("pre_sq"), 1)

            def root(t):
                act.wait_ge(*stage("pre_var", s, t + 1))
                act.activation(std[:, t:t + 1], var[:, t:t + 1], ACT.Sqrt).then_inc(sig("pre_std"), 1)

            def high(u):
                t, half = divmod(u, 2)
                act.wait_ge(*stage("pre_tr", s, u + 1))
                act.activation(dst_hi[:, 4 * half:4 * half + 4, P * t:P * t + P],
                               ps[banks[u % len(banks)]][:, :].rearrange("p (k n) -> p k n", k=4),
                               ACT.Copy).then_inc(sig("pre_hi"), 1)
            return square, root, high

        def run(*steps):
            for f, at in steps:
                f(at)

        def pre_norm_act(act, s, src, scrap, tile_ready, dst_hi, banks):
            sq, root, high = pre_act(act, s, src, scrap, tile_ready, dst_hi, banks)
            run((sq, 0), (sq, 1), (root, 0), (sq, 2), (root, 1), (high, 0), (high, 1), (sq, 3), (root, 2), (high, 2),
                (high, 3), (root, 3), (high, 4), (high, 5), (high, 6), (high, 7))

        def pre_norm_dve(dve, s, src, hn, g, dst_hi, dst_lo, banks, apply):
            def variance(t):
                dve.wait_ge(*stage("pre_sq", s, t + 1))
                nc.vector.tensor_scalar(var[:, t:t + 1], ssq[:, t:t + 1], 1.0 / D, RMS_EPS, ALU.mult, ALU.add)\
                    .then_inc(sig("pre_var"), 1)

            def normed(t):
                dve.wait_ge(*stage("pre_std", s, t + 1))
                nc.vector.reciprocal(rstd[:, t:t + 1], std[:, t:t + 1]).then_inc(sig("pre_rstd"), 1)
                dve.wait_ge(*stage("pre_rstd", s, t + 1))
                if t == 0:
                    gain_wait(dve, g)
                if t >= 2:
                    dve.wait_ge(*stage("pre_tr", s, 2 * (t - 1)))
                nc.vector.scalar_tensor_tensor(hn[:, t % 2, :], src[:, t, :], rstd[:, t:t + 1], gain[g % 2][:, :],
                                               ALU.mult, ALU.mult).then_inc(sig("pre_hn"), 1)

            def low(u):
                t, half = divmod(u, 2)
                dve.wait_ge(*stage("pre_hi", s, u + 1))
                block_hi = dst_hi[:, 4 * half:4 * half + 4, P * t:P * t + P]
                nc.vector.tensor_tensor(dst_lo[:, 4 * half:4 * half + 4, P * t:P * t + P],
                                        ps[banks[u % len(banks)]][:, :].rearrange("p (k n) -> p k n", k=4),
                                        block_hi.bitcast(F32), ALU.subtract).then_inc(sig("pre_lo"), 1)
            run((apply, 0), (apply, 1), (variance, 0), (apply, 2), (normed, 0), (variance, 1), (apply, 3), (normed, 1),
                (variance, 2), (low, 0), (low, 1), (normed, 2), (variance, 3), (low, 2), (low, 3), (normed, 3),
                (low, 4), (low, 5), (low, 6), (low, 7))

        def pre_norm_pe(pe, s, tiles, hn, banks):
            for u in range(2 * tiles[0], 2 * tiles[-1] + 2):
                t, half = divmod(u, 2)
                pe.wait_ge(*stage("pre_hn", s, t + 1))
                if u >= len(banks):
                    pe.wait_ge(*stage("pre_lo", s, u - len(banks) + 1))
                for k in range(4):
                    last = nc.tensor.transpose(ps[banks[u % len(banks)]][:, P * k:P * k + P],
                                               hn[:, t % 2, P * (4 * half + k):P * (4 * half + k) + P], ident[:, :])
                last.then_inc(sig("pre_tr"), 1)

        def post_squares_act(act, s, scrap, used, half):
            act.wait_ge(sig("panel_used"), used[half])
            for t in range(NT):
                if half or t:
                    act.wait_ge(*stage("post_sq", s, NT * half + t))
                act.activation(scrap, ps[4 * half + t][:, :], ACT.Square,
                               accum_out=ssq[:, NT * half + t:NT * half + t + 1]).then_inc(sig("post_sq"), 1)

        def warm_sqrt(act):
            act.activation(scrap1[:, 0:1], ident[:, 0:1], ACT.Sqrt)

        def post_norm_act(act, s, scrap, used):
            post_squares_act(act, s, scrap, used, 0)
            warm_sqrt(act)
            post_squares_act(act, s, scrap, used, 1)
            act.wait_ge(*stage("post_var", s, 2))
            act.activation(std[:, NT:2 * NT], var[:, NT:2 * NT], ACT.Sqrt).then_inc(sig("post_std"), 1)

        def post_copies_dve(dve, s, yb, half, g):
            gain_wait(dve, g)
            for t in range(NT):
                dve.wait_ge(*stage("post_sq", s, NT * half + t + 1))
                nc.vector.tensor_tensor(yb[:, t, T * half:T * half + T], ps[4 * half + t][:, :],
                                        gain[g % 2][:, T * half:T * half + T], ALU.mult).then_inc(sig("post_out"), 1)

        def post_apply_dve(dve, s, yb):
            nc.vector.tensor_tensor(var[:, 0:NT], ssq[:, 0:NT], ssq[:, NT:2 * NT], ALU.add)\
                .then_inc(sig("post_var"), 1)
            dve.wait_ge(*stage("post_var", s, 1))
            nc.vector.tensor_scalar(var[:, NT:2 * NT], var[:, 0:NT], 1.0 / D, RMS_EPS, ALU.mult, ALU.add)\
                .then_inc(sig("post_var"), 1)
            dve.wait_ge(*stage("post_std", s, 1))
            nc.vector.reciprocal(rstd[:, NT:2 * NT], std[:, NT:2 * NT]).then_inc(sig("post_rstd"), 1)
            dve.wait_ge(*stage("post_rstd", s, 1))
            dve.wait_ge(*stage("post_out", s, 2 * NT))

            def apply(t):
                nc.vector.scalar_tensor_tensor(xt[:, t, :], yb[:, t, :], rstd[:, NT + t:NT + t + 1], xt[:, t, :],
                                               ALU.mult, ALU.add).then_inc(sig("x_new"), 1)
            return apply

        def fm_panel(pe, p, slot, bank, a_hi_, a_lo_, n):
            pe.wait_ge(sig("panel_split"), p + 1)
            for k in range(KT):
                hi, lo = w_hi[slot][:, P * k:P * k + P], w_lo[slot][:, P * k:P * k + P]
                nc.tensor.matmul(ps[bank][:, 0:n], hi, a_hi_[:, k, 0:n], start=(k == 0), stop=False)
                nc.tensor.matmul(ps[bank][:, 0:n], hi, a_lo_[:, k, 0:n], start=False, stop=False)
                last = nc.tensor.matmul(ps[bank][:, 0:n], lo, a_hi_[:, k, 0:n], start=False, stop=(k == KT - 1))
            last.then_inc(sig("panel_used"), 1)

        def tm_panel(pe, p, slot, banks, a_hi_, a_lo_, pair, pairs, width):
            pe.wait_ge(sig("panel_split"), p + 1)
            for kk in range(2):
                k = 2 * pair + kk
                hi, lo = w_hi[slot][:, width * kk:width * kk + width], w_lo[slot][:, width * kk:width * kk + width]
                for t, bank in enumerate(banks):
                    o = ps[bank][:, 0:width]
                    xh, xl = a_hi_[:, k, P * t:P * t + P], a_lo_[:, k, P * t:P * t + P]
                    nc.tensor.matmul(o, xh, hi, start=(k == 0), stop=False)
                    nc.tensor.matmul(o, xh, lo, start=False, stop=False)
                    last = nc.tensor.matmul(o, xl, hi, start=False, stop=(k == 2 * pairs - 1))
            last.then_inc(sig("panel_used"), 1)

        block = ctx.enter_context(nc.Block())

        @block.sync
        def _(sp_eng):
            for t in range(NT):
                sp_eng.dma_start(xt[:, t, :], x[0, P * t:P * t + P, :]).then_inc(sig(f"x_loaded{t}"), 16)

            def fetch(p, slot, src, width=P, rows=KT):
                if not (type(p) is int and p < 2):
                    sp_eng.wait_ge(sig("panel_split"), p - 1)
                sp_eng.dma_start(raw[slot][:, 0:rows * width].rearrange("p (k n) -> p k n", k=rows), src)\
                    .then_inc(sig(f"raw_loaded{slot}"), 16)

            panel_run(sp_eng, P_A, A_TILES, 2, lambda j, p, slot, use: fetch(p, slot, fm_cols(w_in, P * j)))
            for j in range(Q_TILES):
                fetch(P_Q + j, (P_Q + j) % 2, fm_cols(w_in, q_col(j)))
            for j in range(KT // 2):
                fetch(P_VB + j, (P_VB + j) % 2, tm_rows(w_in, j, A_COLS + 2 * BW, VB_W), VB_W, 2)
            for j in range(KT // 2):
                fetch(P_VC + j, (P_VC + j) % 2, tm_rows(w_in, j, A_COLS + B_COLS + 2 * CW, VC_W), VC_W, 2)
            for j in range(KT):
                fetch(P_WO + j, (P_WO + j) % 2, tm_rows(w_out, j % 4, T * (j // 4), T), T, 2)
            panel_run(sp_eng, P_MK, KT, 2, lambda j, p, slot, use: fetch(p, slot, fm_cols(mem_wkv, P * j)))
            for j in range(KT):
                fetch(P_MV + j, (P_MV + j) % 2, tm_rows(mem_wkv, j % 4, D + T * (j // 4), T), T, 2)
            panel_run(sp_eng, P_MQ, KT, 2, lambda j, p, slot, use: fetch(p, slot, fm_cols(mem_wq, P * j)))
            for j in range(KT):
                fetch(P_MO + j, (P_MO + j) % 2, tm_rows(mem_wo, j % 4, T * (j // 4), T), T, 2)
            gu = ffn_w_gu[0].rearrange("(k p) (h n) -> p k h n", p=P, h=2)
            with sp_eng.Fori(0, FT) as f:
                for s in range(2):
                    fetch(P_GU + s + 2 * f, (P_GU + s) % 2, gu[:, :, s, bass.ds(P * f, P)])
            for j in range(FT):
                fetch(P_DN + j, (P_DN + j) % 2, tm_rows(ffn_w_down, j % (FT // 2), T * (j // (FT // 2)), T), T, 2)
            for t in range(NT):
                sp_eng.wait_ge(*stage("x_new", 3, t + 1))
                sp_eng.dma_start(out[0, P * t:P * t + P, :], xt[:, t, :]).then_inc(sig("stored"), 16)
            sp_eng.wait_ge(sig("stored"), 16 * NT)

        @block.gpsimd
        def _(pool):
            own = Steps(pool, sig("constant_steps"))
            step = own.step

            def keep(tile, pattern, base, cm, op, other=0.0):
                own.sync()
                step(nc.gpsimd.affine_select(out=tile, in_=tile, compare_op=op, fill=other, base=base,
                                             pattern=pattern, channel_multiplier=cm))

            def fill(tile, value):
                own.sync()
                step(nc.gpsimd.memset(tile, value))

            step(nc.gpsimd.memset(ident[:, :], 0.0))
            fill(zraw[:, :, 0:1], 0.0)
            keep(ident[:, :], [[-1, P]], 0, 1, ALU.not_equal, 1.0)
            own.sync()
            nc.gpsimd.memset(pair_ones[:, :], 0.0).then_inc(sig("ident_ready"), 1)
            pool.wait_ge(sig("ident_ready"), 1)
            fill(pair_ones[0:HD, 0:HD], 1.0)
            fill(pair_ones[HD:P, HD:P], 1.0)
            fill(grams[:, :], 1.0)
            gv = grams[:, :].rearrange("p (a b j) -> p a b j", a=2, b=2)
            keep(gv[:, 0], [[CHUNK, 2], [1, CHUNK]], 0, -1, ALU.is_gt)
            keep(gv[:, 1], [[CHUNK, 2], [1, CHUNK]], 0, -1, ALU.is_ge)
            keep(gv, [[0, 2], [-CHUNK, 2], [0, CHUNK]], 0, 1, ALU.is_ge)
            fill(lowm[:, :], 0.0)
            keep(lowm[:, 0:P:2], [[-2, P // 2]], -1, 1, ALU.not_equal, 1.0)
            fill(lowmT[:, :], 0.0)
            keep(lowmT[:, :], [[-1, P]], 0, 1, ALU.not_equal, 1.0)
            keep(lowmT[:, 1:P:2], [[-2, P // 2]], 0, 1, ALU.not_equal, 1.0)
            fill(levm[:, :, :], 1.0)
            for n, m in enumerate(LEVELS):
                nb = P // (2 * m)
                v = levm[:, n, :].rearrange("p (b j) -> p b j", b=nb)
                keep(v, [[-2 * m, nb], [0, 2 * m]], -m, 1, ALU.is_ge)
                keep(v, [[2 * m, nb], [0, 2 * m]], 2 * m - 1, -1, ALU.is_ge)
                keep(v, [[0, nb], [-1, 2 * m]], m - 1, 0, ALU.is_ge)
                keep(levm[:, n, :], [[-1, P]], 0, 1, ALU.not_equal, 1.0)
            fill(stack_id[:, :], 0.0)
            keep(stack_id[:, :], [[-1, HD]], 0, 1, ALU.not_equal, 1.0)
            keep(stack_id[:, :], [[-1, HD]], -HD, 1, ALU.not_equal, 1.0)
            fill(tri_ones[:, :], 1.0)
            keep(tri_ones[:, :], [[1, T]], 0, -1, ALU.is_ge)
            fill(nones[:, :], -1.0)
            fill(ntri[:, :], -1.0)
            keep(ntri[:, :], [[-1, P]], 0, 1, ALU.is_ge)
            fill(ident_b[:, :], 0.0)
            keep(ident_b[:, :], [[-1, P]], 0, 1, ALU.not_equal, 1.0)
            fill(fmask_b[:, :], BIG)
            keep(fmask_b[:, :], [[1, P]], 0, -1, ALU.is_gt)
            fill(smask_b[:, :], -BIG)
            keep(smask_b[:, :], [[-1, P]], 0, 1, ALU.is_ge)
            fill(smask[:, :], 1.0)
            keep(smask[:, :], [[1, P]], 0, -1, ALU.is_gt)
            fill(reset[:, :], 1.0)
            own.sync()
            nc.gpsimd.memset(reset[:, 0:T:CHUNK], 0.0).then_inc(sig("constants_ready"), 1)

            def split(p, slot, use, n=D):
                pool.wait_ge(sig(f"raw_loaded{slot}"), 16 * use + 16)
                if not (type(p) is int and p < 2):
                    pool.wait_ge(sig("panel_used"), p - 1)
                pool.sem_inc(sig("slot_open"), 1)
                nc.gpsimd.tensor_scalar(w_hi[slot][:, 0:n], raw[slot][:, 0:n], 1.0, 1.0, ALU.mult, ALU.mult)\
                    .then_inc(sig("panel_high"), 1)
                pool.wait_ge(sig("panel_high"), p + 1)
                nc.gpsimd.tensor_tensor(w_lo[slot][:, 0:n], raw[slot][:, 0:n], w_hi[slot][:, 0:n].bitcast(F32),
                                        ALU.subtract).then_inc(sig("panel_split"), 1)

            panel_run(pool, 0, P_VB, 2, lambda j, p, slot, use: split(p, slot, use))
            for p in range(P_VB, P_WO):
                split(p, p % 2, p // 2, 2 * (VB_W if p < P_VC else VC_W))
            panel_run(pool, P_WO, P_END - P_WO, 2, lambda j, p, slot, use: split(p, slot, use))

        FOX = [(h, i) for h in range(BH) for i in range(NT)]
        STK = [(h, NT - 1 - e) for h in range(CH) for e in range(NT)]

        def row_bank(n, per=NT):
            h, e = divmod(n, per)
            return 2 * (h % 2) + e % 2

        def bank_before(n, per=NT):
            for m in range(n - 1, -1, -1):
                if row_bank(m, per) == row_bank(n, per):
                    return m
            return None

        def half(h):
            return slice(HD * (h % 2), HD * (h % 2) + HD)

        def level_steps(n, g, which):
            last = len(LEVELS) - 1
            if n < last:
                return 4 * n + 2 * g + which
            return 4 * n + g + 1
        N_TE = level_steps(len(LEVELS) - 1, 1, 2)


        MEMU = [(h, i) for h in range(MH) for i in range(NT)]

        def pe_memory(pe):
            mm = nc.tensor.matmul
            pe.wait_ge(*stage("post_out", 1, NT))
            pre_norm_pe(pe, "m", range(MT), hn2, [0, 1])
            for j in range(KT):
                if j < 2:
                    pe.wait_ge(*stage("pre_lo", "m", 2 * MT))
                else:
                    pe.wait_ge(sig("mk_out"), j - 1)
                fm_panel(pe, P_MK + j, (P_MK + j) % 2, j % 2, mem_hi, mem_lo, ML)
            pe.wait_ge(*stage("post_out", 1, 2 * NT))
            pre_norm_pe(pe, 1, range(2), hn2, [6, 7])
            for j in range(KT):
                tm_panel(pe, P_MV + j, (P_MV + j) % 2, [2, 3] if j < 4 else [4, 5], mem_hi, mem_lo, j % 4, 4, T)
            pre_norm_pe(pe, 1, range(2, NT), hn2, [6, 7])
            pe.wait_ge(sig("mk_out"), KT)
            pe.wait_ge(*stage("pre_lo", 1, 2 * NT))
            for j in range(KT):
                if j >= 2:
                    pe.wait_ge(sig("mq_out"), j - 1)
                fm_panel(pe, P_MQ + j, (P_MQ + j) % 2, j % 2, act_hi, act_lo, T)
            pe.wait_ge(sig("mv_out"), 2 * MT)
            pe.wait_ge(sig("mq_out"), KT)

            def scores(n):
                h, i = MEMU[n]
                if n >= 2:
                    pe.wait_ge(sig("mem_exp"), n - 1)
                for k in range(2):
                    last = mm(ps[2 + n % 2][:, 0:ML], mq[:, 2 * h + k, P * i:P * i + P], mk[:, 2 * h + k, :],
                              start=(k == 0), stop=(k == 1))
                last.then_inc(sig("mem_mm"), 1)

            def transposes(n):
                pe.wait_ge(sig("mem_norm"), n + 1)
                if n >= 2:
                    pe.wait_ge(sig("mem_pt"), n - 1)
                for k in range(MT):
                    last = nc.tensor.transpose(ps[4 + n % 2][:, P * k:P * k + P], mp[:, n % 2, P * k:P * k + P], ident[:, :])
                last.then_inc(sig("mem_tr"), 1)

            def values(h):
                pe.wait_ge(sig("mem_pt"), NT * (h + 1))
                for d in range(2):
                    if h:
                        pe.wait_ge(sig("o_lo"), 2 * (h - 1) + d + 1)
                    for k in range(MT):
                        last = mm(ps[6 + d][:, :], mv[:, k, MHD * h + P * d:MHD * h + P * d + P], mpt[:, h % 2, k, :],
                                  start=(k == 0), stop=(k == MT - 1))
                    last.then_inc(sig("mem_pv"), 1)
            for n in range(len(MEMU) + 3):
                if n < len(MEMU):
                    scores(n)
                if 1 <= n < len(MEMU) + 1:
                    transposes(n - 1)
                if n >= NT + 2 and (n - NT - 2) % NT == 0:
                    values((n - NT - 2) // NT)
            pe.wait_ge(sig("o_lo"), KT)
            for j in range(KT):
                tm_panel(pe, P_MO + j, (P_MO + j) % 2, [0, 1, 2, 3] if j < 4 else [4, 5, 6, 7], act_hi, act_lo, j % 4, 4, T)

        def act_memory(act, A):
            for t in range(MT):
                act.dma_start(mx[:, t, :], mem[0, P * t:P * t + P, :]).then_inc(sig(f"mem_loaded{t}"), 16)
            for t in range(MT):
                act.wait_ge(sig(f"mem_loaded{t}"), 16)
                if t:
                    act.wait_ge(*stage("pre_sq", "m", t))
                act.activation(junk2[:, :], mx[:, t, :], ACT.Square, accum_out=ssq2[:, t:t + 1]).then_inc(sig("pre_sq"), 1)
            for t in range(MT):
                act.wait_ge(*stage("pre_var", "m", t + 1))
                A(ssq2[:, 4 + t:5 + t], ssq2[:, 2 + t:3 + t], ACT.Sqrt).then_inc(sig("pre_std"), 1)
            post_squares_act(act, 1, junk2[:, 0:T], (P_WO + 4, P_WO + 8), 0)
            for u in range(2 * MT):
                t, half_ = divmod(u, 2)
                act.wait_ge(*stage("pre_tr", "m", u + 1))
                A(mem_hi[:, 4 * half_:4 * half_ + 4, P * t:P * t + P], ps[u % 2][:, :].rearrange("p (k n) -> p k n", k=4),
                  ACT.Copy).then_inc(sig("pre_hi"), 1)
            gain_wait(act, 1)
            act.wait_ge(*stage("pre_hn", "m", MT))
            gain_load(act, 3)
            post_squares_act(act, 1, junk2[:, 0:T], (P_WO + 4, P_WO + 8), 1)
            def keys(j):
                act.wait_ge(sig("panel_used"), P_MK + j + 1)
                A(mk[:, j, :], ps[j % 2][:, 0:ML], ACT.Copy).then_inc(sig("mk_out"), 1)
            act.wait_ge(*stage("post_var", 1, 2))
            A(std[:, NT:2 * NT], var[:, NT:2 * NT], ACT.Sqrt).then_inc(sig("post_std"), 1)
            act.wait_ge(*stage("post_out", 1, 2 * NT))
            gain_load(act, 4)
            sq, root, high = pre_act(act, 1, xt, junk2[:, :], lambda t: stage("x_new", 1, t + 1), act_hi, [6, 7])

            def values(half_):
                act.wait_ge(sig("panel_used"), P_MV + 4 * half_ + 4)
                for t in range(MT):
                    A(mv[:, t, T * half_:T * half_ + T], ps[2 + 2 * half_ + t][:, :], ACT.Copy).then_inc(sig("mv_out"), 1)
            run((keys, 0), (keys, 1), (sq, 0), (keys, 2), (sq, 1), (root, 0), (keys, 3), (sq, 2), (root, 1), (keys, 4),
                (sq, 3), (keys, 5), (root, 2), (keys, 6), (keys, 7), (high, 0), (high, 1), (high, 2), (high, 3),
                (root, 3), (values, 0), (values, 1), (high, 4), (high, 5), (high, 6), (high, 7))
            act.wait_ge(*stage("pre_hn", 1, NT))
            gain_load(act, 5)
            for j in range(KT):
                act.wait_ge(sig("panel_used"), P_MQ + j + 1)
                A(mq[:, j, :], ps[j % 2][:, :], ACT.Copy, scale=-(MHD ** -0.5)).then_inc(sig("mq_out"), 1)

            def exps(n):
                act.wait_ge(sig("mem_min"), n + 1)
                if n >= 2:
                    act.wait_ge(sig("mem_tr"), n - 1)
                A(mp[:, n % 2, :], ps[2 + n % 2][:, 0:ML], ACT.Exp, bias=msm[:, n % 4, 0:1], scale=-1.0,
                  accum_out=msm[:, n % 4, 1:2]).then_inc(sig("mem_exp"), 1)

            def pts(n):
                h, i = MEMU[n]
                act.wait_ge(sig("mem_tr"), n + 1)
                if i == 0 and h >= 2:
                    act.wait_ge(sig("mem_pv"), 2 * (h - 1))
                A(mpt[:, h % 2, :, P * i:P * i + P], ps[4 + n % 2][:, 0:ML].rearrange("p (k n) -> p k n", k=MT), ACT.Copy)\
                    .then_inc(sig("mem_pt"), 1)

            def o_high(h):
                for d in range(2):
                    act.wait_ge(sig("mem_pv"), 2 * h + d + 1)
                    A(act_hi[:, 2 * h + d, :], ps[6 + d][:, :], ACT.Copy).then_inc(sig("o_hi"), 1)
            for n in range(len(MEMU) + 3):
                if n < len(MEMU):
                    exps(n)
                if 1 <= n < len(MEMU) + 1:
                    pts(n - 1)
                if n >= NT + 2 and (n - NT - 2) % NT == 0:
                    o_high((n - NT - 2) // NT)
            post_norm_act(act, 2, junk2[:, 0:T], (P_MO + 4, P_MO + 8))

        def dve_memory(dve, V):
            for t in range(MT):
                dve.wait_ge(*stage("pre_sq", "m", t + 1))
                V.tensor_scalar(ssq2[:, 2 + t:3 + t], ssq2[:, t:t + 1], 1.0 / D, RMS_EPS, ALU.mult, ALU.add)\
                    .then_inc(sig("pre_var"), 1)
            for t in range(MT):
                dve.wait_ge(*stage("pre_std", "m", t + 1))
                V.reciprocal(ssq2[:, 6 + t:7 + t], ssq2[:, 4 + t:5 + t]).then_inc(sig("pre_rstd"), 1)
            dve.wait_ge(*stage("pre_rstd", "m", MT))
            gain_wait(dve, 1)
            for t in range(MT):
                V.scalar_tensor_tensor(hn2[:, t, :], mx[:, t, :], ssq2[:, 6 + t:7 + t], gain[1][:, :], ALU.mult, ALU.mult)\
                    .then_inc(sig("pre_hn"), 1)
            post_copies_dve(dve, 1, ybuf, 0, 2)
            for u in range(2 * MT):
                t, half_ = divmod(u, 2)
                dve.wait_ge(*stage("pre_hi", "m", u + 1))
                block_hi = mem_hi[:, 4 * half_:4 * half_ + 4, P * t:P * t + P]
                V.tensor_tensor(mem_lo[:, 4 * half_:4 * half_ + 4, P * t:P * t + P],
                                ps[u % 2][:, :].rearrange("p (k n) -> p k n", k=4), block_hi.bitcast(F32), ALU.subtract)\
                    .then_inc(sig("pre_lo"), 1)
            post_copies_dve(dve, 1, ybuf, 1, 2)
            pre_norm_dve(dve, 1, xt, hn2, 3, act_hi, act_lo, [6, 7], post_apply_dve(dve, 1, ybuf))

            def minimum(n):
                dve.wait_ge(sig("mem_mm"), n + 1)
                if n >= 4:
                    dve.wait_ge(sig("mem_exp"), n - 3)
                V.tensor_reduce(out=msm[:, n % 4, 0:1], in_=ps[2 + n % 2][:, 0:ML], op=ALU.min, axis=AX.X)\
                    .then_inc(sig("mem_min"), 1)

            def norm(n):
                dve.wait_ge(sig("mem_exp"), n + 1)
                V.reciprocal(msm[:, n % 4, 2:3], msm[:, n % 4, 1:2]).then_inc(sig("mem_recip"), 1)
                dve.wait_ge(sig("mem_recip"), n + 1)
                V.tensor_scalar(mp[:, n % 2, :], mp[:, n % 2, :], msm[:, n % 4, 2:3], None, ALU.mult).then_inc(sig("mem_norm"), 1)

            def o_low(h):
                for d in range(2):
                    dve.wait_ge(sig("o_hi"), 2 * h + d + 1)
                    V.tensor_tensor(act_lo[:, 2 * h + d, :], ps[6 + d][:, :], act_hi[:, 2 * h + d, :].bitcast(F32),
                                    ALU.subtract).then_inc(sig("o_lo"), 1)
            for n in range(len(MEMU) + 3):
                if n < len(MEMU):
                    minimum(n)
                    norm(n)
                if n >= NT + 2 and (n - NT - 2) % NT == 0:
                    o_low((n - NT - 2) // NT)
            post_copies_dve(dve, 2, ybuf, 0, 4)
            post_copies_dve(dve, 2, ybuf, 1, 4)

        def pe_ffn(pe):
            pe.wait_ge(*stage("post_out", 2, 2 * NT))
            pre_norm_pe(pe, 2, range(NT), hn2, [0, 1, 2, 3])
            pe.wait_ge(*stage("pre_lo", 2, 2 * NT))
            for f in range(2):
                for s in range(2):
                    fm_panel(pe, P_GU + 2 * f + s, (P_GU + s) % 2, 4 + 2 * f + s, act_hi, act_lo, T)
            with pe.Fori(0, FT // 2 - 1) as turn:
                for f in range(2):
                    pe.wait_ge(sig("ffn_prod"), 2 * turn + f + 1)
                    for s in range(2):
                        fm_panel(pe, P_GU + 4 + 2 * f + s + 4 * turn, (P_GU + s) % 2, 4 + 2 * f + s, act_hi, act_lo, T)
            for half_ in range(2):
                for j in range(FT // 2):
                    p = P_DN + FT // 2 * half_ + j
                    if half_ == 0 and j == 0:
                        pe.wait_ge(sig("ffn_lo"), FT - 2)
                    if half_ == 0 and j == FT // 2 - 1:
                        pe.wait_ge(sig("ffn_lo"), FT)
                    if half_ == 1 and j == 0:
                        pe.wait_ge(sig("ffn_prod"), FT)
                    tm_panel(pe, p, p % 2, [4 * half_ + t for t in range(NT)], a_hi, a_lo, j, FT // 2, T)

        def act_ffn(act, A):
            pre_norm_act(act, 2, xt, junk2[:, :], lambda t: stage("x_new", 2, t + 1), act_hi, [0, 1, 2, 3])
            act.wait_ge(*stage("pre_hn", 2, NT))
            gain_load(act, 6)

            def unit(f, b):
                act.wait_ge(sig("panel_used"), P_GU + 1 + 2 * f)
                A(ftmp[:, b, :], ps[4 + 2 * b][:, :], ACT.Sigmoid).then_inc(sig("ffn_sig"), 1)
                act.wait_ge(sig("ffn_prod"), 1 + f)
                A(a_hi[:, bass.ds(f, 1), :], ftmp[:, 2 + b, :].unsqueeze(1), ACT.Copy).then_inc(sig("ffn_hi"), 1)
            unit(0, 0)
            unit(1, 1)
            with act.Fori(0, FT // 2 - 1) as turn:
                for b in range(2):
                    unit(2 + b + 2 * turn, b)
            post_norm_act(act, 3, junk_f[:, :], (P_DN + FT // 2, P_END))

        def dve_ffn(dve, V):
            pre_norm_dve(dve, 2, xt, hn2, 5, act_hi, act_lo, [0, 1, 2, 3], post_apply_dve(dve, 2, ybuf))

            def unit(f, b):
                dve.wait_ge(sig("ffn_sig"), 1 + f)
                V.tensor_tensor(ftmp[:, 2 + b, :], ps[4 + 2 * b][:, :], ftmp[:, b, :], ALU.mult).then_inc(sig("ffn_silu"), 1)
                dve.wait_ge(sig("ffn_silu"), 1 + f)
                dve.wait_ge(sig("panel_used"), P_GU + 2 + 2 * f)
                V.tensor_tensor(ftmp[:, 2 + b, :], ps[5 + 2 * b][:, :], ftmp[:, 2 + b, :], ALU.mult).then_inc(sig("ffn_prod"), 1)
                dve.wait_ge(sig("ffn_hi"), 1 + f)
                V.tensor_tensor(a_lo[:, bass.ds(f, 1), :], ftmp[:, 2 + b, :].unsqueeze(1),
                                a_hi[:, bass.ds(f, 1), :].bitcast(F32), ALU.subtract).then_inc(sig("ffn_lo"), 1)
            unit(0, 0)
            unit(1, 1)
            with dve.Fori(0, FT // 2 - 1) as turn:
                for b in range(2):
                    unit(2 + b + 2 * turn, b)
            post_copies_dve(dve, 3, ybuf, 0, 6)
            post_copies_dve(dve, 3, ybuf, 1, 6)
            apply = post_apply_dve(dve, 3, ybuf)
            for t in range(NT):
                apply(t)

        @block.tensor
        def _(pe):
            mm = nc.tensor.matmul
            pe.wait_ge(sig("ident_ready"), 1)
            pre_norm_pe(pe, 0, range(NT), hn, [0, 1, 2, 3])
            pe.wait_ge(sig("small_loaded"), SMALL_LOADS)
            nc.tensor.transpose(ps[7][:, 0:V_ROWS], vec_rows[:, :], ident[0:V_ROWS, 0:V_ROWS]).then_inc(sig("vecs_ps"), 1)

            def in_panel(j, p, slot, use):
                if type(p) is int and p < 2:
                    pe.wait_ge(*stage("pre_lo", 0, 2 * NT))
                else:
                    pe.wait_ge(sig("w_in_out"), p - 1)
                fm_panel(pe, p, slot, slot, act_hi, act_lo, T)
            panel_run(pe, 0, P_VB, 2, in_panel)
            pe.wait_ge(sig("vecs_ready"), 1)
            for j in range(KT // 2):
                tm_panel(pe, P_VB + j, (P_VB + j) % 2, [4, 5, 6, 7], act_hi, act_lo, j, KT // 2, VB_W)

            pe.wait_ge(sig("w_in_out"), P_VB)
            pe.wait_ge(sig("lora_in"), 2)
            pe.wait_ge(sig("small_loaded"), SMALL_LOADS)
            for c in range(APAIRS):
                cols = slice(P * c, P * c + P)
                for n, (w, a) in enumerate(((lora_w[0:LORA, cols], z[0:LORA, A_TILES - 2, :]),
                                            (lora_w[LORA:P, cols], z[LORA:P, A_TILES - 2, :]),
                                            (gate_w[:, cols], z[:, A_TILES - 1, :]))):
                    if c:
                        pe.wait_ge(sig("lora_out"), 3 * (c - 1) + n + 1)
                    mm(ps[n][:, :], w, a, start=True, stop=True).then_inc(sig("lora_mm"), 1)
            pe.wait_ge(sig("constants_ready"), 1)
            for c in range(APAIRS):
                pe.wait_ge(sig("kk_squared"), c + 1)
                if c:
                    pe.wait_ge(sig("kk_max"), c)
                mm(ps[3][:, :], pair_ones[:, :], clog[:, c, :], start=True, stop=True).then_inc(sig("kk_sums"), 1)
            pe.wait_ge(sig("vB_out"), NT)
            for j in range(KT // 2):
                tm_panel(pe, P_VC + j, (P_VC + j) % 2, [4, 5, 6, 7], act_hi, act_lo, j, KT // 2, VC_W)

            def fox_scores(n):
                h, i = FOX[n]
                if i == 0:
                    if h == 0:
                        pe.wait_ge(sig("lf_ready"), 1)
                        pe.wait_ge(sig("vC_out"), NT)
                    else:
                        pe.wait_ge(sig("cb_out"), h)
                    for s in range(NT):
                        last = mm(ps[7][:, P * s:T], lf[:, s, h:h + 1].to_broadcast([P, P]), tri_ones[:, 0:T - P * s],
                                  start=(s == 0), stop=(s == NT - 1))
                    last.then_inc(sig("cb_mm"), 1)
                b, w = row_bank(n), P * (i + 1)
                if bank_before(n) is not None:
                    pe.wait_ge(sig("fox_min"), bank_before(n) + 1)
                elif n < 2:
                    pe.wait_ge(sig("lora_out"), 3 * APAIRS)
                else:
                    pe.wait_ge(sig("kk_max"), APAIRS)
                mm(ps[b][:, 0:w], qk[half(h), h // 2, P * i:w], qk[half(h), APAIRS + h // 2, 0:w], start=True, stop=False)
                mm(ps[b][:, P * i:w], ident_b[:, :], fmask_b[:, :], start=False, stop=True).then_inc(sig("fox_mm"), 1)

            def fox_transpose(n):
                h, i = FOX[n]
                pe.wait_ge(sig("fox_norm"), n + 1)
                if n >= 2:
                    pe.wait_ge(sig("fox_pt"), n - 1)
                for j in range(i + 1):
                    last = nc.tensor.transpose(ps[4 + n % 2][:, P * j:P * j + P], fp[:, n % 3, P * j:P * j + P], ident[:, :])
                last.then_inc(sig("fox_tr"), 1)

            def fox_values(n):
                h, i = FOX[n]
                pe.wait_ge(sig("fox_pt"), n + 1)
                if n % (2 * NT) == 0 and n:
                    pe.wait_ge(sig("y_lo"), n // (2 * NT))
                for j in range(i + 1):
                    last = mm(ps[6][half(h), P * i:P * i + P], vB[:, j, HD * h:HD * h + HD],
                              fpt[:, n % 2, P * j:P * j + P], start=(j == 0), stop=(j == i))
                last.then_inc(sig("fox_pv"), 1)

            for n in range(len(FOX) + 3):
                if n < len(FOX):
                    fox_scores(n)
                if 2 <= n < len(FOX) + 2:
                    fox_transpose(n - 2)
                if n >= 3:
                    fox_values(n - 3)

            def stick_logits(n, bank, stop):
                h, j = STK[n]
                mm(ps[bank][:, 0:NJ[j]], qk[half(h), 2 * APAIRS + CH // 2 + h // 2, P * j:P * j + P],
                   qk[half(h), 2 * APAIRS + h // 2, P * j:T], start=True, stop=stop)\
                    .then_inc(sig("stick_mm" if stop else "stick_again"), 1)

            def stick_sums(n):
                h, j = STK[n]
                pe.wait_ge(sig("stick_sp"), n + 1)
                if n >= 2:
                    pe.wait_ge(sig("stick_exp"), n - 1)
                else:
                    pe.wait_ge(sig("fox_pt"), len(FOX))
                b = 4 + n % 2
                stick_logits(n, b, False)
                mm(ps[b][:, 0:P], ident_b[:, :], smask_b[:, :], start=False, stop=False)
                for j2 in range(j, NT):
                    last = mm(ps[b][:, P * (j2 - j):NJ[j]], (ntri if j2 == j else nones)[:, :],
                              sp[:, h % 2, OJ[j2]:OJ[j2] + NJ[j2]], start=False, stop=(j2 == NT - 1))
                last.then_inc(sig("stick_cum"), 1)

            def stick_values(h):
                pe.wait_ge(sig("stick_exp"), NT * (h + 1))
                if h == 0:
                    pe.wait_ge(sig("y_lo"), APAIRS)
                    pe.wait_ge(sig("cb_out"), BH)
                for j in range(NT):
                    last = mm(ps[6 + h // 2][half(h), P * j:T], vC[:, j, HD * h:HD * h + HD],
                              satt[:, h % 2, OJ[j]:OJ[j] + NJ[j]], start=(j == 0), stop=(j == NT - 1))
                last.then_inc(sig("stick_pv"), 1)

            for n in range(len(STK) + 3):
                if n < len(STK):
                    before = bank_before(n)
                    if before is not None:
                        pe.wait_ge(sig("stick_sp"), before + 1)
                    else:
                        pe.wait_ge(sig("fox_min"), len(FOX))
                    stick_logits(n, row_bank(n), True)
                if 2 <= n < len(STK) + 2:
                    stick_sums(n - 2)
                if n >= NT + 2 and (n - NT - 2) % NT == 0:
                    stick_values((n - NT - 2) // NT)

            HH = [(g, c, 3 * g + c) for g in range(2) for c in range(APAIRS)]
            pe.wait_ge(sig("y_lo"), APAIRS + CH // 2)

            def rwkv_turn(i):
                pe.wait_ge(sig("rw_in"), i + 1)
                pe.wait_ge(sig("rw_vt"), i + 1)
                for kind in range(4):
                    for c in range(APAIRS):
                        src = (AR[:, c, 0, :], BKh[:, 0, c, :], BKh[:, 1, c, :], Vt[:, c, :])[kind]
                        last = nc.tensor.transpose(ps[kind][:, P * c:P * c + P], src, ident[:, :])
                    last.then_inc(sig("rw_tr"), 1)
                for g in range(2):
                    for c in range(APAIRS):
                        last = mm(ps[4 + 2 * g + c // 2][:, 2 * P * (c % 2):2 * P * (c % 2) + 2 * P],
                                  BK[half(g), 0, c, :], AR[half(g), c, :, :], start=True, stop=True)
                        if c:
                            last.then_inc(sig("rw_g1m"), 1)
                for g in range(2):
                    pe.wait_ge(sig("rw_g1"), 4 * i + 2 * g + 2)
                    for c in range(APAIRS):
                        last = mm(ps[4 + 2 * g][:, P * c:P * c + P], AR[half(g), c, 0, :], BK[half(g), 0, c, :],
                                  start=True, stop=True)
                    last.then_inc(sig("rw_nm"), 1)
                pe.wait_ge(sig("rw_tok"), 4 * i + 4)
                for g in range(2):
                    for c in range(APAIRS):
                        last = mm(ps[2 * g + c // 2][:, 2 * P * (c % 2):2 * P * (c % 2) + 2 * P],
                                  BK[half(g), 1, c, :], AR[half(g), c, :, :], start=True, stop=True)
                        if c:
                            last.then_inc(sig("rw_g2m"), 1)
                pe.wait_ge(sig("rw_g2"), 4 * i + 4)
                for g, c, hh in HH:
                    last = mm(ps[6][:, HD * hh:HD * hh + HD], G2[:, hh, 0:P], tokV[:, hh, :], start=True, stop=True)
                last.then_inc(sig("rw_avm"), 1)
                for n in range(len(LEVELS)):
                    for g in range(2):
                        if n == 0:
                            pe.wait_ge(sig("rw_t2"), i + 1)
                        else:
                            pe.wait_ge(sig("rw_te"), N_TE * i + level_steps(n - 1, g, 2))
                        for c in range(APAIRS):
                            last = mm(ps[g][:, P * c:P * c + P], G1[:, 3 * g + c, 0:P], Tm[:, 3 * g + c, :],
                                      start=True, stop=True)
                        last.then_inc(sig("rw_xm"), 1)
                    for g in range(2):
                        pe.wait_ge(sig("rw_x"), 2 * len(LEVELS) * i + 2 * n + g + 1)
                        if n < len(LEVELS) - 1:
                            for c in range(APAIRS):
                                last = mm(ps[2 + g][:, P * c:P * c + P], TT[:, 3 * g + c, :], X[:, 3 * g + c, :],
                                          start=True, stop=True)
                            last.then_inc(sig("rw_tm"), 1)
                        for c in range(APAIRS):
                            last = mm(ps[4 + g][:, P * c:P * c + P], X[:, 3 * g + c, :], TT[:, 3 * g + c, :],
                                      start=True, stop=True)
                        last.then_inc(sig("rw_tm"), 1)
                pe.wait_ge(sig("rw_rhs"), i + 1)
                for g in range(2):
                    pe.wait_ge(sig("rw_te"), N_TE * i + level_steps(len(LEVELS) - 1, g, 2))
                    for c in range(APAIRS):
                        last = mm(ps[g][:, P * c:P * c + P], TT[:, 3 * g + c, :], RHS[:, 3 * g + c, :],
                                  start=True, stop=True)
                    last.then_inc(sig("rw_wum"), 1)
                pe.wait_ge(sig("rw_wu"), 2 * i + 2)
                for g, c, hh in HH:
                    last = mm(ps[7][half(g), P * c:P * c + P], WU[:, hh, 0:HD], G1[:, hh, P:2 * P], start=True, stop=True)
                last.then_inc(sig("rw_gtm"), 1)
                for ch in range(2):
                    rows = half(ch)
                    for g, c, hh in HH:
                        mm(ps[2 + ch][half(g), HD * c:HD * c + HD], WU[rows, hh, 0:HD], tokBK[rows, 0, hh, :],
                           start=True, stop=True)
                    for g, c, hh in HH:
                        o = ps[2 + ch][half(g), HD * (APAIRS + c):HD * (APAIRS + c) + HD]
                        mm(o, tokBK[rows, 0, hh, :], WU[rows, hh, HD:P], start=True, stop=False)
                        last = mm(o, tokBK[rows, 1, hh, :], tokV[rows, hh, :], start=False, stop=True)
                    last.then_inc(sig("rw_pqm"), 1)
                for ch in range(2):
                    pe.wait_ge(sig("rw_pt"), 4 * i + 2 * ch + 2)
                    pe.wait_ge(sig("rw_state"), 3 * i + ch + 1)
                    for c in range(APAIRS):
                        last = mm(ps[4][:, HD * c:HD * c + HD], PT[:, ch, c, :], St[:, ch, c, :], start=True, stop=True)
                    last.then_inc(sig("rw_sm"), 1)
                    if ch == 0:
                        for g, c, hh in HH:
                            o = ps[5][half(g), P * c:P * c + P]
                            mm(o, WU[:, hh, HD:P], G1[:, hh, P:2 * P], start=True, stop=False)
                            last = mm(o, tokV[:, hh, :], G2[:, hh, P:2 * P], start=False, stop=True)
                        last.then_inc(sig("rw_yhm"), 1)
                pe.wait_ge(sig("rw_gt"), i + 1)
                pe.wait_ge(sig("rw_sbd"), 4 * i + 4)
                for ch in range(2):
                    for c in range(APAIRS):
                        last = mm(ps[6][:, P * c + HD * ch:P * c + HD * ch + HD], Sbd[:, ch, c, :],
                                  GT[:, c, HD * ch:HD * ch + HD], start=True, stop=True)
                last.then_inc(sig("rw_ygm"), 1)
            with pe.Fori(0, NT) as i:
                rwkv_turn(i)

            pe.wait_ge(sig("rw_y"), NT)
            for c in range(APAIRS):
                mm(ps[c][:, :], pair_ones[:, :], Y[:, c, :], start=True, stop=True).then_inc(sig("gn_sum"), 1)
            for c in range(APAIRS):
                pe.wait_ge(sig("bonus_in"), c + 1)
                mm(ps[6][:, :] if c == 0 else ps[6 + c % 2][:, :], pair_ones[:, :], yq[:, c, 2, :], start=True, stop=True)\
                    .then_inc(sig("bonus_sum"), 1)
                if c == 1:
                    pe.wait_ge(sig("bonus_out"), 1)
            for c in range(APAIRS):
                pe.wait_ge(sig("gn_sq"), c + 1)
                mm(ps[3 + c][:, :], pair_ones[:, :], yq[:, c, 0, :], start=True, stop=True).then_inc(sig("gn_var"), 1)

            pe.wait_ge(sig("y_lo"), KT)
            for j in range(KT):
                tm_panel(pe, P_WO + j, (P_WO + j) % 2, [0, 1, 2, 3] if j < 4 else [4, 5, 6, 7], act_hi, act_lo, j % 4, 4, T)
            pe_memory(pe)
            pe_ffn(pe)

        @block.scalar
        def _(act_eng):
            act, A = act_eng, nc.scalar.activation
            small = [(vec_rows[V_MU:V_W0, :], shift_mu.rearrange("a (t p) -> (a t) p", p=P))]
            for at, v in ((V_W0, rwkv_w0), (V_A0, rwkv_a0), (V_KK, rwkv_k_k), (V_KA, rwkv_k_a), (V_GG, rwkv_gn_g),
                          (V_GB, rwkv_gn_b)):
                small.append((vec_rows[at:at + APAIRS, :], v.rearrange("a (t p) -> (a t) p", p=P)))
            small.append((vec_rows[V_RK:V_RK + APAIRS, :], rwkv_r_k.rearrange("a (t h) d -> (a t) (h d)", h=2)))
            small += [(lora_w[0:LORA, :], rwkv_w_up[0]), (lora_w[LORA:P, :], rwkv_a_up[0]), (gate_w[:, :], rwkv_g_up[0]),
                      (fbias[:, :], fox_f_bias[0].partition_broadcast(P))]
            assert 16 * len(small) == SMALL_LOADS
            gain_load(act, 0)
            for to, src in small:
                act.dma_start(to, src).then_inc(sig("small_loaded"), 16)
            gain_load(act, 1)
            pre_norm_act(act, 0, xt, junk[:, :], lambda t: (sig(f"x_loaded{t}"), 16), act_hi, [0, 1, 2, 3])
            act.wait_ge(*stage("pre_hn", 0, NT))
            gain_load(act, 2)
            for j in range(P_VB):
                act.wait_ge(sig("panel_used"), j + 1)
                if j < A_TILES:
                    if j >= 2:
                        act.wait_ge(sig("z_ready"), j - 1)
                    A(zraw[:, j % 2, 1:T + 1], ps[j % 2][:, :], ACT.Copy).then_inc(sig("w_in_out"), 1)
                else:
                    q = j - A_TILES
                    scale = -HD ** -0.5 if q < BW // P else HD ** -0.5 if 2 * BW // P <= q < (2 * BW + CW) // P else 1.0
                    A(qk[:, q, :], ps[j % 2][:, :], ACT.Copy, scale=scale).then_inc(sig("w_in_out"), 1)
            act.wait_ge(sig("z_ready"), A_TILES)
            A(z[0:LORA, A_TILES - 2, :], z[0:LORA, A_TILES - 2, :], ACT.Tanh).then_inc(sig("lora_in"), 1)
            A(z[:, A_TILES - 1, :], z[:, A_TILES - 1, :], ACT.Sigmoid).then_inc(sig("lora_in"), 1)
            act.wait_ge(sig("panel_used"), P_VC)
            for t in range(NT):
                A(vB[:, t, :], ps[4 + t][:, 0:VB_W], ACT.Copy).then_inc(sig("vB_out"), 1)
            for c in range(APAIRS):
                act.wait_ge(sig("lora_mm"), 3 * c + 1)
                A(sigw[:, c, :], ps[0][:, :], ACT.Sigmoid, bias=vecs[:, V_W0 + c:V_W0 + c + 1]).then_inc(sig("lora_out"), 1)
                act.wait_ge(sig("lora_mm"), 3 * c + 2)
                A(kka[:, c, :], ps[1][:, :], ACT.Sigmoid, bias=vecs[:, V_A0 + c:V_A0 + c + 1]).then_inc(sig("lora_out"), 1)
                act.wait_ge(sig("lora_mm"), 3 * c + 3)
                A(gate[:, c, :], ps[2][:, :], ACT.Copy).then_inc(sig("lora_out"), 1)
            for c in range(APAIRS):
                act.wait_ge(sig("kk_max"), c + 1)
                A(zs[:, c, :], zs[:, c, :], ACT.Sqrt).then_inc(sig("kk_norm"), 1)
            act.wait_ge(sig("panel_used"), P_WO)
            for t in range(NT):
                A(vC[:, t, :], ps[4 + t][:, 0:VC_W], ACT.Copy).then_inc(sig("vC_out"), 1)
            act.wait_ge(sig("lf_sum"), 1)
            A(lf2[:, :, :], lf[:, :, :], ACT.Abs).then_inc(sig("lf_exp"), 1)
            act.wait_ge(sig("lf_exp"), 1)
            A(lf2[:, :, :], lf2[:, :, :], ACT.Exp, scale=-1.0).then_inc(sig("lf_exp"), 1)
            act.wait_ge(sig("lf_exp"), 2)
            A(lf2[:, :, :], lf2[:, :, :], ACT.Ln, bias=1.0).then_inc(sig("lf_exp"), 1)

            def y_high(n, src, bank_ready):
                act.wait_ge(*bank_ready)
                A(act_hi[:, n, :], src, ACT.Copy).then_inc(sig("y_hi"), 1)

            def fox_exp(n):
                h, i = FOX[n]
                w = P * (i + 1)
                act.wait_ge(sig("fox_min"), n + 1)
                if n >= 3:
                    act.wait_ge(sig("fox_tr"), n - 2)
                A(fp[:, n % 3, 0:w], fs[:, n % 3, 0:w], ACT.Exp, bias=small_t[:, n % 4, 0:1], scale=-1.0,
                  accum_out=small_t[:, n % 4, 1:2]).then_inc(sig("fox_exp"), 1)

            def fox_pt(n):
                h, i = FOX[n]
                w = P * (i + 1)
                act.wait_ge(sig("fox_tr"), n + 1)
                if n >= 2:
                    act.wait_ge(sig("fox_pv"), n - 1)
                A(fpt[:, n % 2, 0:w], ps[4 + n % 2][:, 0:w], ACT.Copy).then_inc(sig("fox_pt"), 1)

            for n in range(len(FOX) + 3):
                if n < len(FOX):
                    h, i = FOX[n]
                    if i == 0:
                        act.wait_ge(sig("cb_mm"), h + 1)
                        if h >= 2:
                            act.wait_ge(sig("fox_min"), NT * (h - 1))
                        A(cb[:, h % 2, :], ps[7][:, :], ACT.Copy).then_inc(sig("cb_out"), 1)
                    fox_exp(n)
                if 2 <= n < len(FOX) + 2:
                    fox_pt(n - 2)
                if n >= 3 and (n - 3) % (2 * NT) == 2 * NT - 1:
                    c = (n - 3) // (2 * NT)
                    y_high(APAIRS + c, ps[6][:, :], (sig("fox_pv"), 2 * NT * (c + 1)))

            def stick_softplus(n):
                h, j = STK[n]
                w = NJ[j]
                act.wait_ge(sig("stick_mm"), n + 1)
                if n >= 2:
                    act.wait_ge(sig("stick_sp"), n - 1)
                t = se[:, n % 2, 0:w]
                A(t, ps[row_bank(n)][:, 0:w], ACT.Abs).then_inc(sig("stick_abs"), 1)
                act.wait_ge(sig("stick_abs"), 3 * n + 1)
                A(t, t, ACT.Exp, scale=-1.0).then_inc(sig("stick_abs"), 1)
                act.wait_ge(sig("stick_abs"), 3 * n + 2)
                A(t, t, ACT.Ln, bias=1.0).then_inc(sig("stick_abs"), 1)

            def stick_exp(n):
                h, j = STK[n]
                act.wait_ge(sig("stick_cum"), n + 1)
                if h >= 2:
                    act.wait_ge(sig("stick_pv"), h - 1)
                A(satt[:, h % 2, OJ[j]:OJ[j] + NJ[j]], ps[4 + n % 2][:, 0:NJ[j]], ACT.Exp).then_inc(sig("stick_exp"), 1)

            act.wait_ge(sig("fox_min"), len(FOX))
            act.wait_ge(sig("fox_pv"), len(FOX))
            for n in range(len(STK) + 3):
                if n < len(STK):
                    stick_softplus(n)
                if 2 <= n < len(STK) + 2:
                    stick_exp(n - 2)
                if n >= NT + 2 and (n - NT - 2) % (2 * NT) == NT:
                    c = (n - NT - 2) // (2 * NT)
                    y_high(2 * APAIRS + c, ps[6 + c][:, :], (sig("stick_pv"), 2 * c + 2))

            act.wait_ge(sig("rw_zero"), 3)
            with act.Fori(0, NT) as i:
                now = bass.ds(P * i, P)
                act.wait_ge(sig("rw_state"), 3 * i + 1)
                A(E[:, 0], clog[:, :, now], ACT.Exp, scale=-DECAY_C).then_inc(sig("rw_E"), 1)
                A(E[:, 1], clog[:, :, now], ACT.Exp, scale=DECAY_C).then_inc(sig("rw_E"), 1)
                act.wait_ge(sig("rw_lp"), i + 1)
                A(E[:, 2], lp[:, :, :], ACT.Exp, scale=-DECAY_C).then_inc(sig("rw_E"), 1)
                A(Vt[:, :, :], z[:, 2 * APAIRS:3 * APAIRS, now], ACT.Copy).then_inc(sig("rw_vt"), 1)
                for kind in range(4):
                    act.wait_ge(sig("rw_tr"), 4 * i + kind + 1)
                    to = (RHS[:, :, 0:HD], tokBK[:, 0], tokBK[:, 1], tokV[:, :, :])[kind]
                    A(to.rearrange("p (g c) d -> p c g d", g=2),
                      ps[kind][:, 0:AW].rearrange("p (c g d) -> p c g d", c=APAIRS, g=2), ACT.Copy).then_inc(sig("rw_tok"), 1)
                act.wait_ge(sig("rw_avm"), i + 1)
                A(RHS[:, :, HD:P], ps[6][:, 0:AW].rearrange("p (h d) -> p h d", h=AH), ACT.Copy).then_inc(sig("rw_rhs"), 1)
                three = "p (c n) -> p c n"
                for n in range(len(LEVELS)):
                    for g in range(2):
                        for which in ((1, 2) if n < len(LEVELS) - 1 else (2,)):
                            act.wait_ge(sig("rw_tm"), N_TE * i + level_steps(n, g, which))
                            A((Tm if which == 1 else TT)[:, 3 * g:3 * g + 3, :],
                              ps[2 * which + g][:, 0:AW].rearrange(three, c=3), ACT.Copy).then_inc(sig("rw_te"), 1)
                for g in range(2):
                    act.wait_ge(sig("rw_wum"), 2 * i + g + 1)
                    A(WU[:, 3 * g:3 * g + 3, :], ps[g][:, 0:AW].rearrange(three, c=3), ACT.Copy).then_inc(sig("rw_wu"), 1)
                for ch in range(2):
                    act.wait_ge(sig("rw_pqm"), 2 * i + ch + 1)
                    A(QS[:, ch], ps[2 + ch][:, AW // 2:AW].rearrange(three, c=3), ACT.Copy).then_inc(sig("rw_q"), 1)
                act.wait_ge(sig("rw_yhm"), i + 1)
                A(Y[:, :, now], ps[5][:, 0:AW].rearrange(three, c=3), ACT.Copy).then_inc(sig("rw_yh"), 1)
                for ch in range(2):
                    act.wait_ge(sig("rw_state"), 3 * i + ch + 1)
                    for g in range(2):
                        A(Sbd[half(g), ch, :, HD * g:HD * g + HD], St[half(g), ch], ACT.Copy).then_inc(sig("rw_sbd"), 1)

            for c in range(APAIRS):
                act.wait_ge(sig("gn_eps"), c + 1)
                A(yq[:, c, 0, :], yq[:, c, 0, :], ACT.Sqrt).then_inc(sig("gn_std"), 1)
            for c in range(APAIRS):
                y_high(c, Y[:, c, :], (sig("y_a"), c + 1))
            act_memory(act, A)
            act_ffn(act, A)

        @block.vector
        def _(dve):
            V = nc.vector
            own = Steps(dve, sig("dve_steps"))
            step, sync = own.step, own.sync
            pre_norm_dve(dve, 0, xt, hn, 0, act_hi, act_lo, [0, 1, 2, 3], lambda t: None)
            dve.wait_ge(sig("vecs_ps"), 1)
            V.tensor_copy(vecs[:, :], ps[7][:, 0:V_ROWS]).then_inc(sig("vecs_ready"), 1)
            dve.wait_ge(sig("vecs_ready"), 1)
            for j in range(A_TILES):
                dve.wait_ge(sig("w_in_out"), j + 1)
                now, before = zraw[:, j % 2, 1:T + 1], zraw[:, j % 2, 0:T]
                step(V.tensor_tensor(z[:, j, :], before, now, ALU.subtract))
                sync()
                V.scalar_tensor_tensor(z[:, j, :], z[:, j, :], vecs[:, V_MU + j:V_MU + j + 1], now, ALU.mult, ALU.add)\
                    .then_inc(sig("z_ready"), 1)
            dve.wait_ge(sig("z_ready"), A_TILES)
            step(V.tensor_scalar(omka[:, :], vecs[:, V_KA:V_KA + APAIRS], -1.0, 1.0, ALU.mult, ALU.add))
            for c in range(APAIRS):
                step(V.tensor_scalar(nkk[:, c, :], z[:, APAIRS + c, :], vecs[:, V_KK + c:V_KK + c + 1], None, ALU.mult))
            sync()
            for c in range(APAIRS):
                V.tensor_tensor(clog[:, c, :], nkk[:, c, :], nkk[:, c, :], ALU.mult).then_inc(sig("kk_squared"), 1)
            for c in range(APAIRS):
                dve.wait_ge(sig("kk_sums"), c + 1)
                V.tensor_scalar(zs[:, c, :], ps[3][:, :], 1e-24, None, ALU.max).then_inc(sig("kk_max"), 1)
            dve.wait_ge(sig("lora_out"), 3 * APAIRS)
            for c in range(APAIRS):
                step(V.tensor_scalar(hn[:, c // 2, T * (c % 2):T * (c % 2) + T], kka[:, c, :], vecs[:, V_KA + c:V_KA + c + 1], omka[:, c:c + 1],
                                     ALU.mult, ALU.add))
            sync()
            for c in range(APAIRS):
                step(V.tensor_tensor(z[:, APAIRS + c, :], z[:, APAIRS + c, :], hn[:, c // 2, T * (c % 2):T * (c % 2) + T], ALU.mult))
            for c in range(APAIRS):
                dve.wait_ge(sig("kk_norm"), c + 1)
                step(V.reciprocal(zs[:, c, :], zs[:, c, :]))
            sync()
            for c in range(APAIRS):
                step(V.scalar_tensor_tensor(nkk[:, c, :], nkk[:, c, :], -1.0, zs[:, c, :], ALU.mult, ALU.mult))
            sync()
            for c in range(APAIRS):
                step(V.scalar_tensor_tensor(kka[:, c, :], nkk[:, c, :], -1.0, kka[:, c, :], ALU.mult, ALU.mult))
            dve.wait_ge(sig("constants_ready"), 1)
            for c in range(APAIRS):
                step(V.tensor_tensor_scan(clog[:, c, :], reset[:, :], sigw[:, c, :], 0.0, ALU.mult, ALU.add))
            dve.wait_ge(sig("vB_out"), NT)
            dve.wait_ge(sig("small_loaded"), SMALL_LOADS)
            V.tensor_tensor(lf[:, :, :], vB[:, :, BW:VB_W], fbias[:, :].unsqueeze(1).to_broadcast([P, NT, BH]), ALU.add)\
                .then_inc(sig("lf_sum"), 1)
            dve.wait_ge(sig("lf_exp"), 3)
            V.scalar_tensor_tensor(lf[:, :, :], lf[:, :, :], 0.0, lf2[:, :, :], ALU.min, ALU.subtract)\
                .then_inc(sig("lf_ready"), 1)

            def y_low(n, src):
                dve.wait_ge(sig("y_hi"), (n - APAIRS if n >= APAIRS else n + KT - APAIRS) + 1)
                V.tensor_tensor(act_lo[:, n, :], src, act_hi[:, n, :].bitcast(F32), ALU.subtract).then_inc(sig("y_lo"), 1)

            def fox_min(n):
                h, i = FOX[n]
                w = P * (i + 1)
                dve.wait_ge(sig("fox_mm"), n + 1)
                dve.wait_ge(sig("cb_out"), h + 1)
                if n >= 3:
                    dve.wait_ge(sig("fox_exp"), n - 2)
                V.tensor_tensor_reduce(out=fs[:, n % 3, 0:w], in0=ps[row_bank(n)][:, 0:w], in1=cb[:, h % 2, 0:w],
                                       scale=1.0, scalar=3.0e38, op0=ALU.add, op1=ALU.min,
                                       accum_out=small_t[:, n % 4, 0:1]).then_inc(sig("fox_min"), 1)

            def fox_norm(n):
                h, i = FOX[n]
                w = P * (i + 1)
                dve.wait_ge(sig("fox_exp"), n + 1)
                V.reciprocal(small_t[:, n % 4, 2:3], small_t[:, n % 4, 1:2]).then_inc(sig("fox_recip"), 1)
                dve.wait_ge(sig("fox_recip"), n + 1)
                V.tensor_scalar(fp[:, n % 3, 0:w], fp[:, n % 3, 0:w], small_t[:, n % 4, 2:3], None, ALU.mult)\
                    .then_inc(sig("fox_norm"), 1)

            for n in range(len(FOX) + 3):
                if n < len(FOX):
                    fox_min(n)
                if 1 <= n < len(FOX) + 1:
                    fox_norm(n - 1)
                if n >= 3 and (n - 3) % (2 * NT) == 2 * NT - 1:
                    y_low(APAIRS + (n - 3) // (2 * NT), ps[6][:, :])

            def stick_sp(n):
                h, j = STK[n]
                w = NJ[j]
                dve.wait_ge(sig("stick_abs"), 3 * n + 3)
                if n % NT == 0 and h >= 2:
                    dve.wait_ge(sig("stick_cum"), NT * (h - 1))
                to = sp[:, h % 2, OJ[j]:OJ[j] + w]
                V.scalar_tensor_tensor(to, ps[row_bank(n)][:, 0:w], 0.0, se[:, n % 2, 0:w], ALU.max, ALU.add)\
                    .then_inc(sig("stick_raw"), 1)
                dve.wait_ge(sig("stick_raw"), n + 1)
                V.tensor_tensor(to[:, 0:P], to[:, 0:P], smask[:, :], ALU.mult).then_inc(sig("stick_sp"), 1)

            for n in range(len(STK) + 3):
                if n < len(STK):
                    stick_sp(n)
                if n >= NT + 2 and (n - NT - 2) % (2 * NT) == NT:
                    c = (n - NT - 2) // (2 * NT)
                    y_low(2 * APAIRS + c, ps[6 + c][:, :])

            sync()
            dve.wait_ge(sig("y_lo"), APAIRS + CH // 2)
            V.memset(PT[:, :, :, :], 0.0).then_inc(sig("rw_zero"), 1)
            V.memset(Sbd[:, :, :, :], 0.0).then_inc(sig("rw_zero"), 1)
            V.memset(St[:, 2], 0.0).then_inc(sig("rw_zero"), 1)
            dve.wait_ge(sig("rw_zero"), 3)
            with dve.Fori(0, NT) as i:
                now = bass.ds(P * i, P)
                turn = Steps(dve, sig("rw_dve"), RW_STEPS * i)
                V.tensor_copy(St[:, 0], St[:, 2]).then_inc(sig("rw_state"), 1)
                V.tensor_tensor(lp[:, :, :], clog[:, :, now], sigw[:, :, now], ALU.subtract).then_inc(sig("rw_lp"), 1)
                dve.wait_ge(sig("rw_E"), 3 * i + 2)
                turn.step(V.tensor_tensor(BK[:, 0], kka[:, :, now], E[:, 1], ALU.mult))
                turn.step(V.tensor_tensor(BK[:, 1], z[:, APAIRS:2 * APAIRS, now], E[:, 1], ALU.mult))
                turn.step(V.tensor_tensor(AR[:, :, 1, :], z[:, 0:APAIRS, now], E[:, 0], ALU.mult))
                ends = E[:, 0].rearrange("p c (b j) -> p c b j", b=2)[:, :, :, CHUNK - 1:CHUNK]
                for ch in range(2):
                    turn.step(V.tensor_tensor(Dg[:, ch], stack_id[:, :].unsqueeze(1).to_broadcast([P, APAIRS, HD]),
                                              ends[:, :, ch, :].to_broadcast([P, APAIRS, HD]), ALU.mult))
                turn.sync(2)
                for n in range(2):
                    turn.step(V.tensor_tensor(BKh[:, n].rearrange("p c (b j) -> p c b j", b=2),
                                              BK[:, n].rearrange("p c (b j) -> p c b j", b=2),
                                              ends.to_broadcast([P, APAIRS, 2, CHUNK]), ALU.mult))
                turn.sync()
                dve.wait_ge(sig("rw_E"), 3 * i + 3)
                V.tensor_tensor(AR[:, :, 0, :], nkk[:, :, now], E[:, 2], ALU.mult).then_inc(sig("rw_in"), 1)

                def masked(to, bank, heads, sem):
                    V.tensor_tensor(to, ps[bank][:, 0:2 * P * heads].rearrange("p (h n) -> p h n", h=heads),
                                    grams[:, :].unsqueeze(1).to_broadcast([P, heads, 2 * P]), ALU.mult).then_inc(sem, 1)
                for g in range(2):
                    for b in range(2):
                        dve.wait_ge(sig("rw_g1m"), 4 * i + 2 * g + b + 1)
                        masked(G1[:, 3 * g + 2 * b:3 * g + 2 + b, :], 4 + 2 * g + b, 2 - b, sig("rw_g1"))
                dve.wait_ge(sig("rw_g1"), 4 * i + 4)
                eye = ident[:, :].unsqueeze(1).to_broadcast([P, AH, P])
                turn.step(V.tensor_tensor(G1[:, :, 0:P], G1[:, :, 0:P], eye, ALU.add))
                for g in range(2):
                    dve.wait_ge(sig("rw_nm"), 2 * i + g + 1)
                    turn.step(V.tensor_tensor(Tm[:, 3 * g:3 * g + 3, :], ps[4 + 2 * g][:, 0:AW].rearrange("p (h n) -> p h n", h=3),
                                              lowm[:, :].unsqueeze(1).to_broadcast([P, 3, P]), ALU.mult))
                turn.sync()
                turn.step(V.tensor_tensor(Tm[:, :, :], Tm[:, :, :], eye, ALU.add))
                turn.step(V.tensor_tensor(TT[:, :, :], G1[:, :, 0:P], lowmT[:, :].unsqueeze(1).to_broadcast([P, AH, P]), ALU.mult))
                turn.sync()
                for g in range(2):
                    for b in range(2):
                        dve.wait_ge(sig("rw_g2m"), 4 * i + 2 * g + b + 1)
                        if g == 0 and b == 0:
                            V.nop().then_inc(sig("rw_t2"), 1)
                        masked(G2[:, 3 * g + 2 * b:3 * g + 2 + b, :], 2 * g + b, 2 - b, sig("rw_g2"))
                for n in range(len(LEVELS)):
                    for g in range(2):
                        dve.wait_ge(sig("rw_xm"), 2 * len(LEVELS) * i + 2 * n + g + 1)
                        V.tensor_tensor(X[:, 3 * g:3 * g + 3, :], ps[g][:, 0:AW].rearrange("p (h n) -> p h n", h=3),
                                        levm[:, n, :].unsqueeze(1).to_broadcast([P, 3, P]), ALU.mult).then_inc(sig("rw_x"), 1)
                for ch in range(2):
                    dve.wait_ge(sig("rw_q"), 2 * i + ch + 1)
                    for g in range(2):
                        V.tensor_tensor(PT[half(g), ch, :, HD * g:HD * g + HD],
                                        ps[2 + ch][half(g), 0:AW // 2].rearrange("p (c n) -> p c n", c=3),
                                        Dg[half(g), ch], ALU.add).then_inc(sig("rw_pt"), 1)
                dve.wait_ge(sig("rw_gtm"), i + 1)
                V.tensor_tensor(GT[:, :, :], ps[7][:, 0:AW].rearrange("p (c n) -> p c n", c=3), AR[:, :, 1, :], ALU.add)\
                    .then_inc(sig("rw_gt"), 1)
                for ch in range(2):
                    dve.wait_ge(sig("rw_sm"), 2 * i + ch + 1)
                    V.tensor_tensor(St[:, ch + 1], ps[4][:, 0:AW // 2].rearrange("p (c n) -> p c n", c=3), QS[:, ch], ALU.add)\
                        .then_inc(sig("rw_state"), 1)
                dve.wait_ge(sig("rw_ygm"), i + 1)
                dve.wait_ge(sig("rw_yh"), i + 1)
                dve.wait_ge(sig("rw_state"), 3 * i + 3)
                V.tensor_tensor(Y[:, :, now], ps[6][:, 0:AW].rearrange("p (c n) -> p c n", c=3), Y[:, :, now], ALU.add)\
                    .then_inc(sig("rw_y"), 1)
            fin = Steps(dve, sig("fin_steps"))
            dve.wait_ge(sig("rw_y"), NT)
            for c in range(APAIRS):
                V.scalar_tensor_tensor(yq[:, c, 2, :], z[:, c, :], vecs[:, V_RK + c:V_RK + c + 1], z[:, APAIRS + c, :],
                                       ALU.mult, ALU.mult).then_inc(sig("bonus_in"), 1)
            for c in range(APAIRS):
                dve.wait_ge(sig("gn_sum"), c + 1)
                fin.step(V.scalar_tensor_tensor(Y[:, c, :], ps[c][:, :], -1.0 / HD, Y[:, c, :], ALU.mult, ALU.add))
            fin.sync()
            for c in range(APAIRS):
                V.tensor_tensor(yq[:, c, 0, :], Y[:, c, :], Y[:, c, :], ALU.mult).then_inc(sig("gn_sq"), 1)
            for c in range(APAIRS):
                dve.wait_ge(sig("bonus_sum"), c + 1)
                V.tensor_tensor(yq[:, c, 3, :], ps[6 + c % 2][:, :], z[:, 2 * APAIRS + c, :], ALU.mult)\
                    .then_inc(sig("bonus_out"), 1)
            for c in range(APAIRS):
                dve.wait_ge(sig("gn_var"), c + 1)
                V.tensor_scalar(yq[:, c, 0, :], ps[3 + c][:, :], 1.0 / HD, GN_EPS, ALU.mult, ALU.add).then_inc(sig("gn_eps"), 1)
            for c in range(APAIRS):
                dve.wait_ge(sig("gn_std"), c + 1)
                fin.step(V.reciprocal(yq[:, c, 1, :], yq[:, c, 0, :]))
            fin.sync()
            for c in range(APAIRS):
                fin.step(V.tensor_tensor(Y[:, c, :], Y[:, c, :], yq[:, c, 1, :], ALU.mult))
            fin.sync()
            for c in range(APAIRS):
                fin.step(V.tensor_scalar(Y[:, c, :], Y[:, c, :], vecs[:, V_GG + c:V_GG + c + 1], vecs[:, V_GB + c:V_GB + c + 1],
                                         ALU.mult, ALU.add))
            fin.sync()
            dve.wait_ge(sig("bonus_out"), APAIRS)
            for c in range(APAIRS):
                fin.step(V.tensor_tensor(Y[:, c, :], Y[:, c, :], yq[:, c, 3, :], ALU.add))
            fin.sync()
            for c in range(APAIRS):
                V.tensor_tensor(Y[:, c, :], Y[:, c, :], gate[:, c, :], ALU.mult).then_inc(sig("y_a"), 1)
            for c in range(APAIRS):
                y_low(c, Y[:, c, :])
            dve_memory(dve, V)
            dve_ffn(dve, V)


_INS = ["x", "mem", "norm_mix_pre", "norm_mix_post", "w_in", "shift_mu", "rwkv_w0", "rwkv_w_up", "rwkv_a0", "rwkv_a_up",
        "rwkv_g_up", "rwkv_k_k", "rwkv_k_a", "rwkv_r_k", "rwkv_gn_g", "rwkv_gn_b", "fox_f_bias", "w_out", "norm_mem_pre",
        "norm_mem_post", "norm_mem_kv", "mem_wq", "mem_wkv", "mem_wo", "norm_ffn_pre", "norm_ffn_post", "ffn_w_gu",
        "ffn_w_down"]


def kernel(**inputs):
    import numpy as _np
    import concourse.bacc as _bacc
    from concourse import mybir as _mybir
    from concourse.bass_utils import run_bass_kernel_spmd as _run

    nc = _bacc.Bacc("TRN2", target_bir_lowering=False, num_devices=1)
    arrays, args = {}, []
    for name in _INS:
        a = _np.ascontiguousarray(inputs[name])
        arrays[f"in_{name}"] = a
        args.append(nc.dram_tensor(f"in_{name}", a.shape, _mybir.dt.from_np(a.dtype), kind="ExternalInput").ap())
    args.append(nc.dram_tensor("out_0", (1, T, D), F32, kind="ExternalOutput").ap())
    hybrid_block(nc, *args)
    r = _run(nc, [arrays], core_ids=[0])
    return r.results[0]["out_0"]
```

```python
import numpy as np
import concourse.bass as bass
from concourse import mybir
from contextlib import ExitStack

F32 = mybir.dt.float32
F32R = mybir.dt.float32r
BF16 = mybir.dt.bfloat16
ALU = mybir.AluOpType
ACT = mybir.ActivationFunctionType
AX = mybir.AxisListType

P = 128
D = 1024
T = 512
NT = T // P
KT = D // P
HD = 64
AH, BH, CH = 6, 6, 4
AW, BW, CW = AH * HD, BH * HD, CH * HD
APAIRS = AH // 2
LORA = 64
A_COLS = 3 * AW + 2 * LORA + 128
B_COLS = 3 * BW + BH
A_TILES = A_COLS // P
Q_TILES = (2 * BW + 2 * CW) // P
VB_W, VC_W = BW + BH, CW
ML = 256
MT = ML // P
MH, MHD = 4, 256
FF = 2816
FT = FF // P
CHUNK = 64
LEVELS = [2, 4, 8, 16, 32]
RMS_EPS = 1e-6
GN_EPS = 64e-5
DECAY_C = float(np.exp(-0.5))
BIG = 1e30
CLIP = 30.0

P_A = 0
P_Q = P_A + A_TILES
P_VB = P_Q + Q_TILES
P_VC = P_VB + KT // 2
P_WO = P_VC + KT // 2
P_MK = P_WO + KT
P_MV = P_MK + KT
P_MQ = P_MV + KT
P_MO = P_MQ + KT
P_GU = P_MO + KT
P_DN = P_GU + 2 * FT
P_END = P_DN + FT
SHARED = P_MQ - P_MK - 2

V_MU = 0
V_W0, V_A0, V_KK, V_KA, V_RK, V_GG, V_GB = (A_TILES + APAIRS * n for n in range(7))
V_ROWS = A_TILES + 7 * APAIRS
SMALL_LOADS = 16 * 12
RW_STEPS = 7
RW_PRE = 6


def panel_run(eng, first, count, unroll, body):
    peeled = 2 if first == 0 else 0
    for j in range(peeled):
        body(j, first + j, (first + j) % 2, (first + j) // 2)
    turns = (count - peeled) // unroll
    done = peeled
    if turns > 1:
        with eng.Fori(0, turns) as turn:
            for s in range(unroll):
                p = first + peeled + s
                body(peeled + s + unroll * turn, p + unroll * turn, p % 2, p // 2 + (unroll // 2) * turn)
        done += turns * unroll
    for j in range(done, count):
        body(j, first + j, (first + j) % 2, (first + j) // 2)


def hybrid_block(nc, x, mem, norm_mix_pre, norm_mix_post, w_in, shift_mu, rwkv_w0, rwkv_w_up, rwkv_a0, rwkv_a_up,
                 rwkv_g_up, rwkv_k_k, rwkv_k_a, rwkv_r_k, rwkv_gn_g, rwkv_gn_b, fox_f_bias, w_out, norm_mem_pre,
                 norm_mem_post, norm_mem_kv, mem_wq, mem_wkv, mem_wo, norm_ffn_pre, norm_ffn_post, ffn_w_gu,
                 ffn_w_down, out):
    ctx = ExitStack()
    with ctx:
        def sb(name, shape, dt=F32, where=ctx):
            return where.enter_context(nc.sbuf_tensor(name, shape, dt))

        sems = {}

        def sig(name):
            if name not in sems:
                sems[name] = ctx.enter_context(nc.semaphore(name))
            return sems[name]

        xt = sb("xt", [P, NT, D])
        operand = ExitStack()
        act_hi = sb("act_hi", [P, KT, T], F32R, where=operand)
        act_lo = sb("act_lo", [P, KT, T], F32R, where=operand)
        operand.close()
        SB_W = sum(T - P * j for j in range(NT))
        se = sb("se", [P, SB_W])
        sb("act_hi_rest", [P, KT * T - SB_W])
        sp0 = sb("sp0", [P, SB_W])
        sb("act_lo_rest", [P, KT * T - SB_W])
        raw = [sb(f"raw{s}", [P, D]) for s in range(2)]
        w_hi = [sb(f"w_hi{s}", [P, D], F32R) for s in range(2)]
        w_lo = [sb(f"w_lo{s}", [P, D], F32R) for s in range(2)]
        gain = [sb(f"gain{b}", [P, D]) for b in range(2)]
        ident = sb("ident", [P, P])
        pair_ones = sb("pair_ones", [P, P])
        vec_rows = sb("vec_rows", [V_ROWS, P])
        vecs = sb("vecs", [P, V_ROWS])
        ssq = sb("ssq", [P, 8])
        var = sb("var", [P, 8])
        std = sb("std", [P, 8])
        rstd = sb("rstd", [P, 8])
        scrap1 = sb("scrap1", [P, 1])

        mix = ExitStack()
        z = sb("z", [P, A_TILES, T], where=mix)
        sigw = sb("sigw", [P, APAIRS, T], where=mix)
        clog = sb("clog", [P, APAIRS, T], where=mix)
        nkk = sb("nkk", [P, APAIRS, T], where=mix)
        kka = sb("kka", [P, APAIRS, T], where=mix)
        gate = sb("gate", [P, APAIRS, T], where=mix)
        lora_w = sb("lora_w", [P, AW], where=mix)
        gate_w = sb("gate_w", [P, AW], where=mix)
        omka = sb("omka", [P, APAIRS], where=mix)
        reset = sb("reset", [P, T], where=mix)
        grams = sb("gram_mask", [P, 2 * P], where=mix)
        lowm = sb("lowm", [P, P], where=mix)
        lowmT = sb("lowmT", [P, P], where=mix)
        levm = sb("levm", [P, len(LEVELS), P], where=mix)
        stack_id = sb("stack_id", [P, HD], where=mix)
        att = ExitStack()
        qk = sb("qk", [P, Q_TILES, T], where=att)
        vB = sb("vB", [P, NT, VB_W], where=att)
        vC = sb("vC", [P, NT, VC_W], where=att)
        tri_ones = sb("tri_ones", [P, T], where=att)
        ntri = sb("ntri", [P, P], where=att)
        nones = sb("nones", [P, P], where=att)
        ident_b = sb("ident_b", [P, P], BF16, where=att)
        fmask_b = sb("fmask_b", [P, P], BF16, where=att)
        smask_b = sb("smask_b", [P, P], BF16, where=att)
        smask = sb("smask", [P, P], where=att)
        lf = sb("lf", [P, NT, BH], where=att)
        lf2 = sb("lf2", [P, NT, BH], where=att)
        fbias = sb("fbias", [P, BH], where=att)
        small_t = sb("small_t", [P, 4, 4], where=att)
        wk_base = ExitStack()
        hn = sb("hn", [P, 2, D], where=wk_base)
        zraw = sb("zraw", [P, 2, T + 8], where=wk_base)
        junk = sb("junk", [P, D], where=wk_base)
        zs = sb("zs", [P, APAIRS, T], where=wk_base)
        wk_base.close()
        fox_ctx = ExitStack()
        cb = sb("cb", [P, 2, T], where=fox_ctx)
        fs = sb("fs", [P, 3, T], where=fox_ctx)
        fp = sb("fp", [P, 3, T], where=fox_ctx)
        fpt = sb("fpt", [P, 2, T], where=fox_ctx)
        fox_ctx.close()
        stick_ctx = ExitStack()
        NJ = [T - P * j for j in range(NT)]
        OJ = [sum(NJ[:j]) for j in range(NT)]
        satt = sb("satt", [P, 2, SB_W], where=stick_ctx)
        sp1 = sb("sp1", [P, SB_W], where=stick_ctx)
        stick_ctx.close()
        sp = [sp0[:, :], sp1[:, :]]
        att.close()
        rw = ExitStack()
        E = sb("E", [P, 3, APAIRS, P], where=rw)
        Rs = sb("Rs", [P, APAIRS, P], where=rw)
        ends = sb("ends", [P, 2, APAIRS, 1], where=rw)
        Vt = sb("Vt", [P, APAIRS, P], where=rw)
        Dg = sb("Dg", [P, 2, APAIRS, HD], where=rw)
        AR = sb("AR", [P, APAIRS, 2, P], where=rw)
        BK = sb("BK", [P, 2, APAIRS, P], where=rw)
        BKh = sb("BKh", [P, 2, APAIRS, P], where=rw)
        tokBK = sb("tokBK", [P, 2, AH, HD], where=rw)
        tokV = sb("tokV", [P, AH, HD], where=rw)
        G1 = sb("G1", [P, AH, 2 * P], where=rw)
        G2 = sb("G2", [P, AH, 2 * P], where=rw)
        Tm = sb("Tm", [P, AH, P], where=rw)
        TT = sb("TT", [P, AH, P], where=rw)
        X = sb("X", [P, AH, P], where=rw)
        RHS = sb("RHS", [P, AH, P], where=rw)
        WU = Tm
        GT = sb("GT", [P, APAIRS, P], where=rw)
        PT = sb("PT", [P, 2, APAIRS, P], where=rw)
        QS = sb("QS", [P, 2, APAIRS, HD], where=rw)
        St = sb("St", [P, 3, APAIRS, HD], where=rw)
        Sbd = sb("Sbd", [P, 2, APAIRS, P], where=rw)
        Y = sb("Y", [P, APAIRS, T], where=rw)
        rw.close()
        fin_ctx = ExitStack()
        yq = sb("yq", [P, APAIRS, 4, T], where=fin_ctx)
        fin_ctx.close()
        mix.close()

        ma = ExitStack()
        ybuf = sb("ybuf", [P, NT, D], where=ma)
        hn2 = sb("hn2", [P, 2, D], where=ma)
        junk2 = sb("junk2", [P, D], where=ma)
        ff = ExitStack()
        a_hi = sb("a_hi", [P, FT, T], F32R, where=ff)
        a_lo = sb("a_lo", [P, FT, T], F32R, where=ff)
        ftmp = sb("ftmp", [P, 4, T], where=ff)
        junk_f = sb("junk_f", [P, T], where=ff)
        ff.close()

        mx = sb("mx", [P, MT, D], where=ma)
        mem_hi = sb("mem_hi", [P, KT, ML], F32R, where=ma)
        mem_lo = sb("mem_lo", [P, KT, ML], F32R, where=ma)
        mk = sb("mk", [P, KT, ML], where=ma)
        mv = sb("mv", [P, MT, D], where=ma)
        mq = sb("mq", [P, KT, T], where=ma)
        mp = sb("mp", [P, 2, ML], where=ma)
        mpt = sb("mpt", [P, 2, MT, T], where=ma)
        msm = sb("msm", [P, 4, 4], where=ma)
        ssq2 = sb("ssq2", [P, 8], where=ma)
        ma.close()

        ps = [ctx.enter_context(nc.psum_tensor(f"ps{b}", [P, T], F32)) for b in range(8)]

        def fm_cols(w, at):
            return w[0].rearrange("(k p) n -> p k n", p=P)[:, :, bass.ds(at, P)]

        def tm_rows(w, pair, at, width):
            return w[0].rearrange("(k p) n -> p k n", p=P)[:, 2 * pair:2 * pair + 2, at:at + width]

        def q_col(j):
            return A_COLS + P * j if j < 2 * BW // P else A_COLS + B_COLS + P * (j - 2 * BW // P)

        class Steps:
            def __init__(self, eng, sem, base=0):
                self.eng, self.sem, self.base, self.n = eng, sem, base, 0

            def step(self, ins):
                ins.then_inc(self.sem, 1)
                self.n += 1
                return self.n

            def sync(self, n=None):
                self.eng.wait_ge(self.sem, self.base + (self.n if n is None else n))

        GAINS = [norm_mix_pre, norm_mem_kv, norm_mix_post, norm_mem_pre, norm_mem_post, norm_ffn_pre, norm_ffn_post]

        def gain_load(eng, g):
            eng.dma_start(gain[g % 2][:, :], GAINS[g][0].partition_broadcast(P)).then_inc(sig(f"gain_loaded{g % 2}"), 16)

        def gain_wait(eng, g):
            eng.wait_ge(sig(f"gain_loaded{g % 2}"), 16 * (g // 2 + 1))

        EACH = {"pre_sq": 1, "pre_hn": 1, "pre_tr": 2, "pre_hi": 2, "pre_lo": 2, "post_sq": 2, "post_out": 2,
                "x_new": 1, "pre_var": 1, "pre_std": 1, "pre_rstd": 1}
        ONCE = {"post_var": 2, "post_std": 1, "post_rstd": 1}

        def stage(name, s, n):
            order = [0, "m", 1, 2] if name.startswith("pre") else [1, 2, 3]
            before = order[:order.index(s)]
            tiles = sum(MT if b == "m" else NT for b in before)
            return sig(name), n + (EACH[name] * tiles if name in EACH else ONCE[name] * len(before))

        def pre_act(act, s, src, scrap, tile_ready, dst_hi, banks):
            def square(t):
                act.wait_ge(*tile_ready(t))
                if t:
                    act.wait_ge(*stage("pre_sq", s, t))
                act.activation(scrap, src[:, t, :], ACT.Square, accum_out=ssq[:, t:t + 1]).then_inc(sig("pre_sq"), 1)

            def root(t):
                act.wait_ge(*stage("pre_var", s, t + 1))
                act.activation(std[:, t:t + 1], var[:, t:t + 1], ACT.Sqrt).then_inc(sig("pre_std"), 1)

            def high(u):
                t, half = divmod(u, 2)
                act.wait_ge(*stage("pre_tr", s, u + 1))
                act.activation(dst_hi[:, 4 * half:4 * half + 4, P * t:P * t + P],
                               ps[banks[u % len(banks)]][:, :].rearrange("p (k n) -> p k n", k=4),
                               ACT.Copy).then_inc(sig("pre_hi"), 1)
            return square, root, high

        def run(*steps):
            for f, at in steps:
                f(at)

        def pre_norm_act(act, s, src, scrap, tile_ready, dst_hi, banks):
            sq, root, high = pre_act(act, s, src, scrap, tile_ready, dst_hi, banks)
            run((sq, 0), (root, 0), (sq, 1), (root, 1), (high, 0), (high, 1), (sq, 2), (root, 2), (high, 2), (high, 3),
                (sq, 3), (root, 3), (high, 4), (high, 5), (high, 6), (high, 7))

        def low_right(dve, n):
            slot = (P_MK + 2 + n) % 2
            dve.wait_ge(sig("panel_high"), P_MK + 3 + n)
            nc.vector.tensor_tensor(w_lo[slot][:, T:D], raw[slot][:, T:D], w_hi[slot][:, T:D].bitcast(F32), ALU.subtract)\
                .then_inc(sig("low_right"), 1)

        def pre_norm_dve(dve, s, src, hn, g, dst_hi, dst_lo, banks, apply):
            def variance(t):
                dve.wait_ge(*stage("pre_sq", s, t + 1))
                nc.vector.tensor_scalar(var[:, t:t + 1], ssq[:, t:t + 1], 1.0 / D, RMS_EPS, ALU.mult, ALU.add)\
                    .then_inc(sig("pre_var"), 1)

            def normed(t):
                dve.wait_ge(*stage("pre_std", s, t + 1))
                nc.vector.reciprocal(rstd[:, t:t + 1], std[:, t:t + 1]).then_inc(sig("pre_rstd"), 1)
                dve.wait_ge(*stage("pre_rstd", s, t + 1))
                if t == 0:
                    gain_wait(dve, g)
                if t >= 2:
                    dve.wait_ge(*stage("pre_tr", s, 2 * (t - 1)))
                nc.vector.scalar_tensor_tensor(hn[:, t % 2, :], src[:, t, :], rstd[:, t:t + 1], gain[g % 2][:, :],
                                               ALU.mult, ALU.mult).then_inc(sig("pre_hn"), 1)

            def low(u):
                t, half = divmod(u, 2)
                dve.wait_ge(*stage("pre_hi", s, u + 1))
                block_hi = dst_hi[:, 4 * half:4 * half + 4, P * t:P * t + P]
                nc.vector.tensor_tensor(dst_lo[:, 4 * half:4 * half + 4, P * t:P * t + P],
                                        ps[banks[u % len(banks)]][:, :].rearrange("p (k n) -> p k n", k=4),
                                        block_hi.bitcast(F32), ALU.subtract).then_inc(sig("pre_lo"), 1)
            if s == 1:
                def share(n):
                    low_right(dve, n)
                run((apply, 0), (share, 0), (apply, 1), (share, 1), (variance, 0), (apply, 2), (share, 2), (normed, 0),
                    (variance, 1), (share, 3), (apply, 3), (normed, 1), (share, 4), (variance, 2), (share, 5), (share, 6),
                    (share, 7), (low, 0), (low, 1), (share, 8), (normed, 2), (variance, 3), (low, 2), (low, 3),
                    (share, 9), (normed, 3), (share, 10), (share, 11), (share, 12), (share, 13),
                    (low, 4), (low, 5), (low, 6), (low, 7))
                return
            run((apply, 0), (apply, 1), (variance, 0), (normed, 0), (apply, 2), (variance, 1), (normed, 1), (apply, 3),
                (low, 0), (low, 1), (variance, 2), (low, 2), (low, 3), (normed, 2), (variance, 3), (normed, 3),
                (low, 4), (low, 5), (low, 6), (low, 7))

        def pre_norm_pe(pe, s, tiles, hn, banks):
            for u in range(2 * tiles[0], 2 * tiles[-1] + 2):
                t, half = divmod(u, 2)
                pe.wait_ge(*stage("pre_hn", s, t + 1))
                if u >= len(banks):
                    pe.wait_ge(*stage("pre_lo", s, u - len(banks) + 1))
                for k in range(4):
                    last = nc.tensor.transpose(ps[banks[u % len(banks)]][:, P * k:P * k + P],
                                               hn[:, t % 2, P * (4 * half + k):P * (4 * half + k) + P], ident[:, :])
                last.then_inc(sig("pre_tr"), 1)

        def post_squares_act(act, s, scrap, used, half):
            act.wait_ge(sig("panel_used"), used[half])
            for t in range(NT):
                if half or t:
                    act.wait_ge(*stage("post_sq", s, NT * half + t))
                act.activation(scrap, ps[4 * half + t][:, :], ACT.Square,
                               accum_out=ssq[:, NT * half + t:NT * half + t + 1]).then_inc(sig("post_sq"), 1)

        def warm_sqrt(act):
            act.activation(scrap1[:, 0:1], ident[:, 0:1], ACT.Sqrt)

        def post_norm_act(act, s, scrap, used):
            post_squares_act(act, s, scrap, used, 0)
            warm_sqrt(act)
            post_squares_act(act, s, scrap, used, 1)
            act.wait_ge(*stage("post_var", s, 2))
            act.activation(std[:, NT:2 * NT], var[:, NT:2 * NT], ACT.Sqrt).then_inc(sig("post_std"), 1)

        def post_copies_dve(dve, s, yb, half, g):
            gain_wait(dve, g)
            for t in range(NT):
                dve.wait_ge(*stage("post_sq", s, NT * half + t + 1))
                nc.vector.tensor_tensor(yb[:, t, T * half:T * half + T], ps[4 * half + t][:, :],
                                        gain[g % 2][:, T * half:T * half + T], ALU.mult).then_inc(sig("post_out"), 1)

        def post_apply_dve(dve, s, yb):
            nc.vector.tensor_tensor(var[:, 0:NT], ssq[:, 0:NT], ssq[:, NT:2 * NT], ALU.add)\
                .then_inc(sig("post_var"), 1)
            dve.wait_ge(*stage("post_var", s, 1))
            nc.vector.tensor_scalar(var[:, NT:2 * NT], var[:, 0:NT], 1.0 / D, RMS_EPS, ALU.mult, ALU.add)\
                .then_inc(sig("post_var"), 1)
            dve.wait_ge(*stage("post_std", s, 1))
            nc.vector.reciprocal(rstd[:, NT:2 * NT], std[:, NT:2 * NT]).then_inc(sig("post_rstd"), 1)
            dve.wait_ge(*stage("post_rstd", s, 1))
            dve.wait_ge(*stage("post_out", s, 2 * NT))

            def apply(t):
                nc.vector.scalar_tensor_tensor(xt[:, t, :], yb[:, t, :], rstd[:, NT + t:NT + t + 1], xt[:, t, :],
                                               ALU.mult, ALU.add).then_inc(sig("x_new"), 1)
            return apply

        def keep_warm(bank, times):
            for _ in range(times):
                nc.tensor.matmul(ps[bank][:, 0:P], ident[:, :], ident[:, :], start=True, stop=True)

        def fm_panel(pe, p, slot, bank, a_hi_, a_lo_, n, at=0, used=True):
            pe.wait_ge(sig("panel_split"), p + 1)
            o = ps[bank][:, at:at + n]
            for k in range(KT):
                hi, lo = w_hi[slot][:, P * k:P * k + P], w_lo[slot][:, P * k:P * k + P]
                nc.tensor.matmul(o, hi, a_hi_[:, k, at:at + n], start=(k == 0), stop=False)
                nc.tensor.matmul(o, hi, a_lo_[:, k, at:at + n], start=False, stop=False)
                last = nc.tensor.matmul(o, lo, a_hi_[:, k, at:at + n], start=False, stop=(k == KT - 1))
            if used:
                last.then_inc(sig("panel_used"), 1)

        def opening(pe, s, hn, norm_banks, first, banks, free_bank=None):
            half_t = T // 2
            if free_bank is not None:
                keep_warm(free_bank, 9)
            pe.wait_ge(*stage("pre_lo", s, NT))
            for n in range(2):
                fm_panel(pe, first + n, (first + n) % 2, banks[n], act_hi, act_lo, half_t, used=False)
                if n == 0:
                    pre_norm_pe(pe, s, range(2, NT), hn, norm_banks)
            pe.wait_ge(*stage("pre_lo", s, 2 * NT))
            for n in range(2):
                fm_panel(pe, first + n, (first + n) % 2, banks[n], act_hi, act_lo, half_t, at=half_t)

        def tm_panel(pe, p, slot, banks, a_hi_, a_lo_, nth, pairs, width, last_first=False):
            pair = pairs - 1 - nth if last_first else nth
            pe.wait_ge(sig("panel_split"), p + 1)
            for kk in range(2):
                k = 2 * pair + kk
                hi, lo = w_hi[slot][:, width * kk:width * kk + width], w_lo[slot][:, width * kk:width * kk + width]
                for t, bank in enumerate(banks):
                    o = ps[bank][:, 0:width]
                    xh, xl = a_hi_[:, k, P * t:P * t + P], a_lo_[:, k, P * t:P * t + P]
                    nc.tensor.matmul(o, xh, hi, start=(nth == 0 and kk == 0), stop=False)
                    nc.tensor.matmul(o, xh, lo, start=False, stop=False)
                    last = nc.tensor.matmul(o, xl, hi, start=False, stop=(nth == pairs - 1 and kk == 1))
            last.then_inc(sig("panel_used"), 1)

        block = ctx.enter_context(nc.Block())

        @block.sync
        def _(sp_eng):
            def load_x(t):
                sp_eng.dma_start(xt[:, t, :], x[0, P * t:P * t + P, :]).then_inc(sig(f"x_loaded{t}"), 16)

            def fetch(p, slot, src, width=P, rows=KT):
                if not (type(p) is int and p < 2):
                    sp_eng.wait_ge(sig("panel_split"), p - 1)
                sp_eng.dma_start(raw[slot][:, 0:rows * width].rearrange("p (k n) -> p k n", k=rows), src)\
                    .then_inc(sig(f"raw_loaded{slot}"), 16)

            load_x(0)
            load_x(1)
            fetch(0, 0, fm_cols(w_in, 0))
            load_x(2)
            load_x(3)
            fetch(1, 1, fm_cols(w_in, P))
            small = [(vec_rows[V_MU:V_W0, :], shift_mu.rearrange("a (t p) -> (a t) p", p=P))]
            for at, v in ((V_W0, rwkv_w0), (V_A0, rwkv_a0), (V_KK, rwkv_k_k), (V_KA, rwkv_k_a), (V_GG, rwkv_gn_g),
                          (V_GB, rwkv_gn_b)):
                small.append((vec_rows[at:at + APAIRS, :], v.rearrange("a (t p) -> (a t) p", p=P)))
            small.append((vec_rows[V_RK:V_RK + APAIRS, :], rwkv_r_k.rearrange("a (t h) d -> (a t) (h d)", h=2)))
            small += [(lora_w[0:LORA, :], rwkv_w_up[0]), (lora_w[LORA:P, :], rwkv_a_up[0]), (gate_w[:, :], rwkv_g_up[0]),
                      (fbias[:, :], fox_f_bias[0].partition_broadcast(P))]
            assert 16 * len(small) == SMALL_LOADS
            for to, src in small:
                sp_eng.dma_start(to, src).then_inc(sig("small_loaded"), 16)
            panel_run(sp_eng, 2, A_TILES - 2, 2, lambda j, p, slot, use: fetch(p, slot, fm_cols(w_in, P * (j + 2))))
            for j in range(Q_TILES):
                fetch(P_Q + j, (P_Q + j) % 2, fm_cols(w_in, q_col(j)))
            for j in range(KT // 2):
                fetch(P_VB + j, (P_VB + j) % 2, tm_rows(w_in, j, A_COLS + 2 * BW, VB_W), VB_W, 2)
            for j in range(KT // 2):
                fetch(P_VC + j, (P_VC + j) % 2, tm_rows(w_in, j, A_COLS + B_COLS + 2 * CW, VC_W), VC_W, 2)
            for j in range(KT):
                fetch(P_WO + j, (P_WO + j) % 2, tm_rows(w_out, 3 - j % 4, T * (j // 4), T), T, 2)
            for j in range(KT):
                if j >= 4:
                    sp_eng.wait_ge(sig("low_right"), j - 3)
                fetch(P_MK + j, (P_MK + j) % 2, fm_cols(mem_wkv, P * j))
            for j in range(KT):
                sp_eng.wait_ge(sig("low_right"), KT + j - 3)
                fetch(P_MV + j, (P_MV + j) % 2, tm_rows(mem_wkv, j % 4, D + T * (j // 4), T), T, 2)
            for j in range(KT):
                if j < 2:
                    sp_eng.wait_ge(sig("low_right"), SHARED - 1 + j)
                fetch(P_MQ + j, (P_MQ + j) % 2, fm_cols(mem_wq, P * j))
            for j in range(KT):
                fetch(P_MO + j, (P_MO + j) % 2, tm_rows(mem_wo, j % 4, T * (j // 4), T), T, 2)
            gu = ffn_w_gu[0].rearrange("(k p) (h n) -> p k h n", p=P, h=2)
            with sp_eng.Fori(0, FT) as f:
                for s in range(2):
                    fetch(P_GU + s + 2 * f, (P_GU + s) % 2, gu[:, :, s, bass.ds(P * f, P)])
            for j in range(FT):
                fetch(P_DN + j, (P_DN + j) % 2, tm_rows(ffn_w_down, j % (FT // 2), T * (j // (FT // 2)), T), T, 2)
            for t in range(NT):
                sp_eng.wait_ge(*stage("x_new", 3, t + 1))
                sp_eng.dma_start(out[0, P * t:P * t + P, :], xt[:, t, :]).then_inc(sig("stored"), 16)
            sp_eng.wait_ge(sig("stored"), 16 * NT)

        @block.gpsimd
        def _(pool):
            own = Steps(pool, sig("constant_steps"))
            step = own.step

            def keep(tile, pattern, base, cm, op, other=0.0):
                own.sync()
                step(nc.gpsimd.affine_select(out=tile, in_=tile, compare_op=op, fill=other, base=base,
                                             pattern=pattern, channel_multiplier=cm))

            def fill(tile, value):
                own.sync()
                step(nc.gpsimd.memset(tile, value))

            def split(p, slot, use, n=D, low_n=None):
                pool.wait_ge(sig(f"raw_loaded{slot}"), 16 * use + 16)
                if not (type(p) is int and p < 2):
                    pool.wait_ge(sig("panel_used"), p - 1)
                pool.sem_inc(sig("slot_open"), 1)
                nc.gpsimd.tensor_scalar(w_hi[slot][:, 0:n], raw[slot][:, 0:n], 1.0, 1.0, ALU.mult, ALU.mult)\
                    .then_inc(sig("panel_high"), 1)
                pool.wait_ge(sig("panel_high"), p + 1)
                m = low_n or n
                nc.gpsimd.tensor_tensor(w_lo[slot][:, 0:m], raw[slot][:, 0:m], w_hi[slot][:, 0:m].bitcast(F32),
                                        ALU.subtract).then_inc(sig("panel_split"), 1)

            step(nc.gpsimd.memset(ident[:, :], 0.0))
            fill(zraw[:, :, 0:1], 0.0)
            keep(ident[:, :], [[-1, P]], 0, 1, ALU.not_equal, 1.0)
            own.sync()
            nc.gpsimd.memset(pair_ones[:, :], 0.0).then_inc(sig("ident_ready"), 1)
            pool.wait_ge(sig("ident_ready"), 1)
            fill(pair_ones[0:HD, 0:HD], 1.0)
            fill(pair_ones[HD:P, HD:P], 1.0)
            fill(grams[:, :], 1.0)
            gv = grams[:, :].rearrange("p (a b j) -> p a b j", a=2, b=2)
            keep(gv[:, 0], [[CHUNK, 2], [1, CHUNK]], 0, -1, ALU.is_gt)
            keep(gv[:, 1], [[CHUNK, 2], [1, CHUNK]], 0, -1, ALU.is_ge)
            keep(gv, [[0, 2], [-CHUNK, 2], [0, CHUNK]], 0, 1, ALU.is_ge)
            fill(lowm[:, :], 0.0)
            keep(lowm[:, 0:P:2], [[-2, P // 2]], -1, 1, ALU.not_equal, 1.0)
            fill(lowmT[:, :], 0.0)
            keep(lowmT[:, :], [[-1, P]], 0, 1, ALU.not_equal, 1.0)
            keep(lowmT[:, 1:P:2], [[-2, P // 2]], 0, 1, ALU.not_equal, 1.0)
            fill(levm[:, :, :], 1.0)
            for n, m in enumerate(LEVELS):
                if n == 2:
                    split(0, 0, 0)
                    split(1, 1, 0)
                nb = P // (2 * m)
                v = levm[:, n, :].rearrange("p (b j) -> p b j", b=nb)
                keep(v, [[-2 * m, nb], [0, 2 * m]], -m, 1, ALU.is_ge)
                keep(v, [[2 * m, nb], [0, 2 * m]], 2 * m - 1, -1, ALU.is_ge)
                keep(v, [[0, nb], [-1, 2 * m]], m - 1, 0, ALU.is_ge)
                keep(levm[:, n, :], [[-1, P]], 0, 1, ALU.not_equal, 1.0)
            for p in (2, 3):
                split(p, p % 2, p // 2)
            fill(stack_id[:, :], 0.0)
            keep(stack_id[:, :], [[-1, HD]], 0, 1, ALU.not_equal, 1.0)
            keep(stack_id[:, :], [[-1, HD]], -HD, 1, ALU.not_equal, 1.0)
            fill(tri_ones[:, :], 1.0)
            keep(tri_ones[:, :], [[1, T]], 0, -1, ALU.is_ge)
            fill(nones[:, :], -1.0)
            fill(ntri[:, :], -1.0)
            keep(ntri[:, :], [[-1, P]], 0, 1, ALU.is_ge)
            for p in (4, 5):
                split(p, p % 2, p // 2)
            fill(ident_b[:, :], 0.0)
            keep(ident_b[:, :], [[-1, P]], 0, 1, ALU.not_equal, 1.0)
            fill(fmask_b[:, :], BIG)
            keep(fmask_b[:, :], [[1, P]], 0, -1, ALU.is_gt)
            fill(smask_b[:, :], -BIG)
            keep(smask_b[:, :], [[-1, P]], 0, 1, ALU.is_ge)
            fill(smask[:, :], 1.0)
            keep(smask[:, :], [[1, P]], 0, -1, ALU.is_gt)
            fill(reset[:, :], 1.0)
            own.sync()
            nc.gpsimd.memset(reset[:, 0:T:CHUNK], 0.0).then_inc(sig("constants_ready"), 1)

            panel_run(pool, 6, P_VB - 6, 2, lambda j, p, slot, use: split(p, slot, use))
            for p in range(P_VB, P_WO):
                split(p, p % 2, p // 2, 2 * (VB_W if p < P_VC else VC_W))
            panel_run(pool, P_WO, P_MK + 2 - P_WO, 2, lambda j, p, slot, use: split(p, slot, use))
            for p in range(P_MK + 2, P_MQ):
                split(p, p % 2, p // 2, low_n=T)
            panel_run(pool, P_MQ, P_END - P_MQ, 2, lambda j, p, slot, use: split(p, slot, use))

        FOX = [(h, i) for h in range(BH) for i in range(NT)]
        STK = [(h, NT - 1 - e) for h in range(CH) for e in range(NT)]

        def row_bank(n, per=NT):
            h, e = divmod(n, per)
            return 2 * (h % 2) + e % 2

        def bank_before(n, per=NT):
            for m in range(n - 1, -1, -1):
                if row_bank(m, per) == row_bank(n, per):
                    return m
            return None

        def half(h):
            return slice(HD * (h % 2), HD * (h % 2) + HD)

        def level_steps(n, g, which):
            last = len(LEVELS) - 1
            if n < last:
                return 4 * n + 2 * g + which
            return 4 * n + g + 1
        N_TE = level_steps(len(LEVELS) - 1, 1, 2)


        MEMU = [(h, i) for h in range(MH) for i in range(NT)]

        def pe_memory(pe):
            mm = nc.tensor.matmul
            pe.wait_ge(*stage("post_out", 1, NT))
            pre_norm_pe(pe, "m", range(MT), hn2, [0, 1])
            for j in range(KT):
                if j < 2:
                    pe.wait_ge(*stage("pre_lo", "m", 2 * MT))
                else:
                    pe.wait_ge(sig("mk_out"), j - 1)
                    pe.wait_ge(sig("low_right"), j - 1)
                fm_panel(pe, P_MK + j, (P_MK + j) % 2, j % 2, mem_hi, mem_lo, ML)
            pe.wait_ge(*stage("post_out", 1, 2 * NT))
            pre_norm_pe(pe, 1, range(2), hn2, [6, 7])
            for j in range(KT):
                pe.wait_ge(sig("low_right"), KT + j - 1)
                tm_panel(pe, P_MV + j, (P_MV + j) % 2, [2, 3] if j < 4 else [4, 5], mem_hi, mem_lo, j % 4, 4, T)
            pe.wait_ge(sig("mk_out"), KT)
            opening(pe, 1, hn2, [6, 7], P_MQ, [0, 1])
            for j in range(2, KT):
                pe.wait_ge(sig("mq_out"), j - 1)
                fm_panel(pe, P_MQ + j, (P_MQ + j) % 2, j % 2, act_hi, act_lo, T)
            pe.wait_ge(sig("mv_out"), 2 * MT)
            pe.wait_ge(sig("mq_out"), KT)

            def scores(n):
                h, i = MEMU[n]
                if n >= 2:
                    pe.wait_ge(sig("mem_exp"), n - 1)
                for k in range(2):
                    last = mm(ps[2 + n % 2][:, 0:ML], mq[:, 2 * h + k, P * i:P * i + P], mk[:, 2 * h + k, :],
                              start=(k == 0), stop=(k == 1))
                last.then_inc(sig("mem_mm"), 1)

            def transposes(n):
                pe.wait_ge(sig("mem_norm"), n + 1)
                if n >= 2:
                    pe.wait_ge(sig("mem_pt"), n - 1)
                for k in range(MT):
                    last = nc.tensor.transpose(ps[4 + n % 2][:, P * k:P * k + P], mp[:, n % 2, P * k:P * k + P], ident[:, :])
                last.then_inc(sig("mem_tr"), 1)

            def values(h):
                pe.wait_ge(sig("mem_pt"), NT * (h + 1))
                for d in range(2):
                    if h:
                        pe.wait_ge(sig("o_lo"), 2 * (h - 1) + d + 1)
                    for k in range(MT):
                        last = mm(ps[6 + d][:, :], mv[:, k, MHD * h + P * d:MHD * h + P * d + P], mpt[:, h % 2, k, :],
                                  start=(k == 0), stop=(k == MT - 1))
                    last.then_inc(sig("mem_pv"), 1)
            for n in range(len(MEMU) + 3):
                if n < len(MEMU):
                    scores(n)
                if 1 <= n < len(MEMU) + 1:
                    transposes(n - 1)
                if n >= NT + 2 and (n - NT - 2) % NT == 0:
                    values((n - NT - 2) // NT)
            pe.wait_ge(sig("o_lo"), KT)
            for j in range(KT):
                tm_panel(pe, P_MO + j, (P_MO + j) % 2, [0, 1, 2, 3] if j < 4 else [4, 5, 6, 7], act_hi, act_lo, j % 4, 4, T)

        def act_memory(act, A):
            for t in range(MT):
                act.dma_start(mx[:, t, :], mem[0, P * t:P * t + P, :]).then_inc(sig(f"mem_loaded{t}"), 16)
            for t in range(MT):
                act.wait_ge(sig(f"mem_loaded{t}"), 16)
                if t:
                    act.wait_ge(*stage("pre_sq", "m", t))
                act.activation(junk2[:, :], mx[:, t, :], ACT.Square, accum_out=ssq2[:, t:t + 1]).then_inc(sig("pre_sq"), 1)
            for t in range(MT):
                act.wait_ge(*stage("pre_var", "m", t + 1))
                A(ssq2[:, 4 + t:5 + t], ssq2[:, 2 + t:3 + t], ACT.Sqrt).then_inc(sig("pre_std"), 1)
            post_squares_act(act, 1, junk2[:, 0:T], (P_WO + 4, P_WO + 8), 0)
            for u in range(2 * MT):
                t, half_ = divmod(u, 2)
                act.wait_ge(*stage("pre_tr", "m", u + 1))
                A(mem_hi[:, 4 * half_:4 * half_ + 4, P * t:P * t + P], ps[u % 2][:, :].rearrange("p (k n) -> p k n", k=4),
                  ACT.Copy).then_inc(sig("pre_hi"), 1)
            gain_wait(act, 1)
            act.wait_ge(*stage("pre_hn", "m", MT))
            gain_load(act, 3)
            post_squares_act(act, 1, junk2[:, 0:T], (P_WO + 4, P_WO + 8), 1)
            def keys(j):
                act.wait_ge(sig("panel_used"), P_MK + j + 1)
                A(mk[:, j, :], ps[j % 2][:, 0:ML], ACT.Copy).then_inc(sig("mk_out"), 1)
            act.wait_ge(*stage("post_var", 1, 2))
            A(std[:, NT:2 * NT], var[:, NT:2 * NT], ACT.Sqrt).then_inc(sig("post_std"), 1)
            act.wait_ge(*stage("post_out", 1, 2 * NT))
            gain_load(act, 4)
            sq, root, high = pre_act(act, 1, xt, junk2[:, :], lambda t: stage("x_new", 1, t + 1), act_hi, [6, 7])

            def values(half_):
                act.wait_ge(sig("panel_used"), P_MV + 4 * half_ + 4)
                for t in range(MT):
                    A(mv[:, t, T * half_:T * half_ + T], ps[2 + 2 * half_ + t][:, :], ACT.Copy).then_inc(sig("mv_out"), 1)
            run((keys, 0), (keys, 1), (sq, 0), (keys, 2), (sq, 1), (root, 0), (keys, 3), (sq, 2), (root, 1), (keys, 4),
                (sq, 3), (keys, 5), (root, 2), (keys, 6), (keys, 7), (high, 0), (high, 1), (high, 2), (high, 3),
                (root, 3), (values, 0), (values, 1), (high, 4), (high, 5), (high, 6), (high, 7))
            act.wait_ge(*stage("pre_hn", 1, NT))
            gain_load(act, 5)
            for j in range(KT):
                act.wait_ge(sig("panel_used"), P_MQ + j + 1)
                A(mq[:, j, :], ps[j % 2][:, :], ACT.Copy, scale=-(MHD ** -0.5)).then_inc(sig("mq_out"), 1)

            def exps(n):
                act.wait_ge(sig("mem_min"), n + 1)
                if n >= 2:
                    act.wait_ge(sig("mem_tr"), n - 1)
                A(mp[:, n % 2, :], ps[2 + n % 2][:, 0:ML], ACT.Exp, bias=msm[:, n % 4, 0:1], scale=-1.0,
                  accum_out=msm[:, n % 4, 1:2]).then_inc(sig("mem_exp"), 1)

            def pts(n):
                h, i = MEMU[n]
                act.wait_ge(sig("mem_tr"), n + 1)
                if i == 0 and h >= 2:
                    act.wait_ge(sig("mem_pv"), 2 * (h - 1))
                A(mpt[:, h % 2, :, P * i:P * i + P], ps[4 + n % 2][:, 0:ML].rearrange("p (k n) -> p k n", k=MT), ACT.Copy)\
                    .then_inc(sig("mem_pt"), 1)

            def o_high(h):
                for d in range(2):
                    act.wait_ge(sig("mem_pv"), 2 * h + d + 1)
                    A(act_hi[:, 2 * h + d, :], ps[6 + d][:, :], ACT.Copy).then_inc(sig("o_hi"), 1)
            for n in range(len(MEMU) + 3):
                if n < len(MEMU):
                    exps(n)
                if 1 <= n < len(MEMU) + 1:
                    pts(n - 1)
                if n >= NT + 2 and (n - NT - 2) % NT == 0:
                    o_high((n - NT - 2) // NT)
            post_norm_act(act, 2, junk2[:, 0:T], (P_MO + 4, P_MO + 8))

        def dve_memory(dve, V):
            for t in range(MT):
                dve.wait_ge(*stage("pre_sq", "m", t + 1))
                V.tensor_scalar(ssq2[:, 2 + t:3 + t], ssq2[:, t:t + 1], 1.0 / D, RMS_EPS, ALU.mult, ALU.add)\
                    .then_inc(sig("pre_var"), 1)
            for t in range(MT):
                dve.wait_ge(*stage("pre_std", "m", t + 1))
                V.reciprocal(ssq2[:, 6 + t:7 + t], ssq2[:, 4 + t:5 + t]).then_inc(sig("pre_rstd"), 1)
            dve.wait_ge(*stage("pre_rstd", "m", MT))
            gain_wait(dve, 1)
            for t in range(MT):
                V.scalar_tensor_tensor(hn2[:, t, :], mx[:, t, :], ssq2[:, 6 + t:7 + t], gain[1][:, :], ALU.mult, ALU.mult)\
                    .then_inc(sig("pre_hn"), 1)
            post_copies_dve(dve, 1, ybuf, 0, 2)
            for u in range(2 * MT):
                t, half_ = divmod(u, 2)
                dve.wait_ge(*stage("pre_hi", "m", u + 1))
                block_hi = mem_hi[:, 4 * half_:4 * half_ + 4, P * t:P * t + P]
                V.tensor_tensor(mem_lo[:, 4 * half_:4 * half_ + 4, P * t:P * t + P],
                                ps[u % 2][:, :].rearrange("p (k n) -> p k n", k=4), block_hi.bitcast(F32), ALU.subtract)\
                    .then_inc(sig("pre_lo"), 1)
            post_copies_dve(dve, 1, ybuf, 1, 2)
            pre_norm_dve(dve, 1, xt, hn2, 3, act_hi, act_lo, [6, 7], post_apply_dve(dve, 1, ybuf))

            def minimum(n):
                dve.wait_ge(sig("mem_mm"), n + 1)
                if n >= 4:
                    dve.wait_ge(sig("mem_exp"), n - 3)
                V.tensor_reduce(out=msm[:, n % 4, 0:1], in_=ps[2 + n % 2][:, 0:ML], op=ALU.min, axis=AX.X)\
                    .then_inc(sig("mem_min"), 1)

            def norm(n):
                dve.wait_ge(sig("mem_exp"), n + 1)
                V.reciprocal(msm[:, n % 4, 2:3], msm[:, n % 4, 1:2]).then_inc(sig("mem_recip"), 1)
                dve.wait_ge(sig("mem_recip"), n + 1)
                V.tensor_scalar(mp[:, n % 2, :], mp[:, n % 2, :], msm[:, n % 4, 2:3], None, ALU.mult).then_inc(sig("mem_norm"), 1)

            def o_low(h):
                for d in range(2):
                    dve.wait_ge(sig("o_hi"), 2 * h + d + 1)
                    V.tensor_tensor(act_lo[:, 2 * h + d, :], ps[6 + d][:, :], act_hi[:, 2 * h + d, :].bitcast(F32),
                                    ALU.subtract).then_inc(sig("o_lo"), 1)
            for n in range(len(MEMU) + 3):
                if n < len(MEMU):
                    minimum(n)
                    norm(n)
                if n >= NT + 2 and (n - NT - 2) % NT == 0:
                    o_low((n - NT - 2) // NT)
            post_copies_dve(dve, 2, ybuf, 0, 4)
            post_copies_dve(dve, 2, ybuf, 1, 4)

        def pe_ffn(pe):
            pe.wait_ge(*stage("post_out", 2, 2 * NT))
            keep_warm(7, 12)
            pre_norm_pe(pe, 2, range(2), hn2, [0, 1, 2, 3])
            opening(pe, 2, hn2, [0, 1, 2, 3], P_GU, [4, 5], 7)
            for s in range(2):
                fm_panel(pe, P_GU + 2 + s, (P_GU + s) % 2, 6 + s, act_hi, act_lo, T)
            with pe.Fori(0, FT // 2 - 1) as turn:
                for f in range(2):
                    pe.wait_ge(sig("ffn_prod"), 2 * turn + f + 1)
                    for s in range(2):
                        fm_panel(pe, P_GU + 4 + 2 * f + s + 4 * turn, (P_GU + s) % 2, 4 + 2 * f + s, act_hi, act_lo, T)
            for half_ in range(2):
                for j in range(FT // 2):
                    p = P_DN + FT // 2 * half_ + j
                    if half_ == 0 and j == 0:
                        pe.wait_ge(sig("ffn_lo"), FT - 2)
                    if half_ == 0 and j == FT // 2 - 1:
                        pe.wait_ge(sig("ffn_lo"), FT)
                    if half_ == 1 and j == 0:
                        pe.wait_ge(sig("ffn_prod"), FT)
                    tm_panel(pe, p, p % 2, [4 * half_ + t for t in range(NT)], a_hi, a_lo, j, FT // 2, T)

        def act_ffn(act, A):
            pre_norm_act(act, 2, xt, junk2[:, :], lambda t: stage("x_new", 2, t + 1), act_hi, [0, 1, 2, 3])
            act.wait_ge(*stage("pre_hn", 2, NT))
            gain_load(act, 6)

            def unit(f, b):
                act.wait_ge(sig("panel_used"), P_GU + 1 + 2 * f)
                A(ftmp[:, b, :], ps[4 + 2 * b][:, :], ACT.Sigmoid).then_inc(sig("ffn_sig"), 1)
                act.wait_ge(sig("ffn_prod"), 1 + f)
                A(a_hi[:, bass.ds(f, 1), :], ftmp[:, 2 + b, :].unsqueeze(1), ACT.Copy).then_inc(sig("ffn_hi"), 1)
            unit(0, 0)
            unit(1, 1)
            with act.Fori(0, FT // 2 - 1) as turn:
                for b in range(2):
                    unit(2 + b + 2 * turn, b)
            post_norm_act(act, 3, junk_f[:, :], (P_DN + FT // 2, P_END))

        def dve_ffn(dve, V):
            pre_norm_dve(dve, 2, xt, hn2, 5, act_hi, act_lo, [0, 1, 2, 3], post_apply_dve(dve, 2, ybuf))

            def unit(f, b):
                dve.wait_ge(sig("ffn_sig"), 1 + f)
                V.tensor_tensor(ftmp[:, 2 + b, :], ps[4 + 2 * b][:, :], ftmp[:, b, :], ALU.mult).then_inc(sig("ffn_silu"), 1)
                dve.wait_ge(sig("ffn_silu"), 1 + f)
                dve.wait_ge(sig("panel_used"), P_GU + 2 + 2 * f)
                V.tensor_tensor(ftmp[:, 2 + b, :], ps[5 + 2 * b][:, :], ftmp[:, 2 + b, :], ALU.mult).then_inc(sig("ffn_prod"), 1)
                dve.wait_ge(sig("ffn_hi"), 1 + f)
                V.tensor_tensor(a_lo[:, bass.ds(f, 1), :], ftmp[:, 2 + b, :].unsqueeze(1),
                                a_hi[:, bass.ds(f, 1), :].bitcast(F32), ALU.subtract).then_inc(sig("ffn_lo"), 1)
            unit(0, 0)
            unit(1, 1)
            with dve.Fori(0, FT // 2 - 1) as turn:
                for b in range(2):
                    unit(2 + b + 2 * turn, b)
            post_copies_dve(dve, 3, ybuf, 0, 6)
            post_copies_dve(dve, 3, ybuf, 1, 6)
            apply = post_apply_dve(dve, 3, ybuf)
            for t in range(NT):
                apply(t)

        @block.tensor
        def _(pe):
            mm = nc.tensor.matmul
            pe.wait_ge(sig("ident_ready"), 1)
            pe.wait_ge(*stage("pre_var", 0, 1))
            keep_warm(6, 7)
            pre_norm_pe(pe, 0, range(2), hn, [2, 3, 4, 5])
            opening(pe, 0, hn, [2, 3, 4, 5], P_A, [0, 1], 6)
            pe.wait_ge(sig("small_loaded"), SMALL_LOADS)
            nc.tensor.transpose(ps[7][:, 0:V_ROWS], vec_rows[:, :], ident[0:V_ROWS, 0:V_ROWS]).then_inc(sig("vecs_ps"), 1)

            def in_panel(j, p, slot, use):
                if type(p) is int and p < 2:
                    return
                pe.wait_ge(sig("w_in_out"), p - 1)
                fm_panel(pe, p, slot, slot, act_hi, act_lo, T)
            panel_run(pe, 0, P_VB, 2, in_panel)
            pe.wait_ge(sig("vecs_ready"), 1)
            for j in range(KT // 2):
                tm_panel(pe, P_VB + j, (P_VB + j) % 2, [4, 5, 6, 7], act_hi, act_lo, j, KT // 2, VB_W)

            pe.wait_ge(sig("w_in_out"), P_VB)
            pe.wait_ge(sig("lora_in"), 2)
            pe.wait_ge(sig("small_loaded"), SMALL_LOADS)
            for c in range(APAIRS):
                cols = slice(P * c, P * c + P)
                for n, (w, a) in enumerate(((lora_w[0:LORA, cols], z[0:LORA, A_TILES - 2, :]),
                                            (lora_w[LORA:P, cols], z[LORA:P, A_TILES - 2, :]),
                                            (gate_w[:, cols], z[:, A_TILES - 1, :]))):
                    if c:
                        pe.wait_ge(sig("lora_out"), 3 * (c - 1) + n + 1)
                    mm(ps[n][:, :], w, a, start=True, stop=True).then_inc(sig("lora_mm"), 1)
            pe.wait_ge(sig("constants_ready"), 1)
            for c in range(APAIRS):
                pe.wait_ge(sig("kk_squared"), c + 1)
                if c:
                    pe.wait_ge(sig("kk_max"), c)
                mm(ps[3][:, :], pair_ones[:, :], clog[:, c, :], start=True, stop=True).then_inc(sig("kk_sums"), 1)
            pe.wait_ge(sig("vB_out"), NT)
            for j in range(KT // 2):
                tm_panel(pe, P_VC + j, (P_VC + j) % 2, [4, 5, 6, 7], act_hi, act_lo, j, KT // 2, VC_W)

            def fox_scores(n):
                h, i = FOX[n]
                if i == 0:
                    if h == 0:
                        pe.wait_ge(sig("lf_ready"), 1)
                        pe.wait_ge(sig("vC_out"), NT)
                    else:
                        pe.wait_ge(sig("cb_out"), h)
                    for s in range(NT):
                        last = mm(ps[7][:, P * s:T], lf[:, s, h:h + 1].to_broadcast([P, P]), tri_ones[:, 0:T - P * s],
                                  start=(s == 0), stop=(s == NT - 1))
                    last.then_inc(sig("cb_mm"), 1)
                b, w = row_bank(n), P * (i + 1)
                if bank_before(n) is not None:
                    pe.wait_ge(sig("fox_min"), bank_before(n) + 1)
                elif n < 2:
                    pe.wait_ge(sig("lora_out"), 3 * APAIRS)
                else:
                    pe.wait_ge(sig("kk_max"), APAIRS)
                mm(ps[b][:, 0:w], qk[half(h), h // 2, P * i:w], qk[half(h), APAIRS + h // 2, 0:w], start=True, stop=False)
                mm(ps[b][:, P * i:w], ident_b[:, :], fmask_b[:, :], start=False, stop=True).then_inc(sig("fox_mm"), 1)

            def fox_transpose(n):
                h, i = FOX[n]
                pe.wait_ge(sig("fox_norm"), n + 1)
                if n >= 2:
                    pe.wait_ge(sig("fox_pt"), n - 1)
                for j in range(i + 1):
                    last = nc.tensor.transpose(ps[4 + n % 2][:, P * j:P * j + P], fp[:, n % 3, P * j:P * j + P], ident[:, :])
                last.then_inc(sig("fox_tr"), 1)

            def fox_values(n):
                h, i = FOX[n]
                pe.wait_ge(sig("fox_pt"), n + 1)
                if n % (2 * NT) == 0 and n:
                    pe.wait_ge(sig("y_lo"), n // (2 * NT))
                for j in range(i + 1):
                    last = mm(ps[6][half(h), P * i:P * i + P], vB[:, j, HD * h:HD * h + HD],
                              fpt[:, n % 2, P * j:P * j + P], start=(j == 0), stop=(j == i))
                last.then_inc(sig("fox_pv"), 1)

            def stick_logits(n, bank, stop):
                h, j = STK[n]
                mm(ps[bank][:, 0:NJ[j]], qk[half(h), 2 * APAIRS + CH // 2 + h // 2, P * j:P * j + P],
                   qk[half(h), 2 * APAIRS + h // 2, P * j:T], start=True, stop=stop)\
                    .then_inc(sig("stick_mm" if stop else "stick_again"), 1)

            def stick_first(n):
                before = bank_before(n)
                if before is not None:
                    pe.wait_ge(sig("stick_over"), before + 1)
                else:
                    pe.wait_ge(sig("fox_min"), len(FOX) - NT - 1 + n)
                stick_logits(n, row_bank(n), True)

            for n in range(len(FOX) + 3):
                if n < len(FOX):
                    fox_scores(n)
                if n == len(FOX) - 3:
                    stick_first(0)
                    stick_first(1)
                if n == len(FOX) - 1:
                    stick_first(2)
                    stick_first(3)
                if 2 <= n < len(FOX) + 2:
                    fox_transpose(n - 2)
                if n >= 3:
                    fox_values(n - 3)

            def stick_sums(n):
                h, j = STK[n]
                pe.wait_ge(sig("stick_sp"), h + 1)
                if n >= 2:
                    pe.wait_ge(sig("stick_exp"), n - 1)
                else:
                    pe.wait_ge(sig("fox_pt"), len(FOX))
                b = 4 + n % 2
                stick_logits(n, b, False)
                mm(ps[b][:, 0:P], ident_b[:, :], smask_b[:, :], start=False, stop=False)
                for j2 in range(j, NT):
                    last = mm(ps[b][:, P * (j2 - j):NJ[j]], (ntri if j2 == j else nones)[:, :],
                              sp[h % 2][:, OJ[j2]:OJ[j2] + NJ[j2]], start=False, stop=(j2 == NT - 1))
                last.then_inc(sig("stick_cum"), 1)

            def stick_values(h):
                pe.wait_ge(sig("stick_exp"), NT * (h + 1))
                if h == 0:
                    pe.wait_ge(sig("y_lo"), APAIRS)
                    pe.wait_ge(sig("cb_out"), BH)
                for j in range(NT):
                    last = mm(ps[6 + h // 2][half(h), P * j:T], vC[:, j, HD * h:HD * h + HD],
                              satt[:, h % 2, OJ[j]:OJ[j] + NJ[j]], start=(j == 0), stop=(j == NT - 1))
                last.then_inc(sig("stick_pv"), 1)

            pe.wait_ge(sig("cb_out"), BH)
            keep_warm(7, 12)
            for h in range(CH):
                if h + 1 < CH:
                    for e in range(NT):
                        stick_first(NT * (h + 1) + e)
                stick_sums(NT * h)
                stick_sums(NT * h + 1)
                if h:
                    stick_values(h - 1)
                stick_sums(NT * h + 2)
                stick_sums(NT * h + 3)
            stick_values(CH - 1)

            HH = [(g, c, 3 * g + c) for g in range(2) for c in range(APAIRS)]
            pe.wait_ge(sig("y_lo"), APAIRS + CH // 2)
            keep_warm(7, 14)

            def rwkv_turn(i):
                pe.wait_ge(sig("rw_in"), i + 1)
                pe.wait_ge(sig("rw_vt"), i + 1)
                for kind in range(4):
                    for c in range(APAIRS):
                        src = (AR[:, c, 0, :], BKh[:, 0, c, :], BKh[:, 1, c, :], Vt[:, c, :])[kind]
                        last = nc.tensor.transpose(ps[kind][:, P * c:P * c + P], src, ident[:, :])
                    last.then_inc(sig("rw_tr"), 1)
                pe.wait_ge(sig("rw_y"), i + 1)
                for g in range(2):
                    for c in range(APAIRS):
                        last = mm(ps[4 + 2 * g + c // 2][:, 2 * P * (c % 2):2 * P * (c % 2) + 2 * P],
                                  BK[half(g), 0, c, :], AR[half(g), c, :, :], start=True, stop=True)
                        if c:
                            last.then_inc(sig("rw_g1m"), 1)
                for g in range(2):
                    pe.wait_ge(sig("rw_g1"), 4 * i + 2 * g + 2)
                    for c in range(APAIRS):
                        last = mm(ps[4 + 2 * g][:, P * c:P * c + P], AR[half(g), c, 0, :], BK[half(g), 0, c, :],
                                  start=True, stop=True)
                    last.then_inc(sig("rw_nm"), 1)
                pe.wait_ge(sig("rw_tok"), 4 * i + 4)
                for g in range(2):
                    for c in range(APAIRS):
                        last = mm(ps[2 * g + c // 2][:, 2 * P * (c % 2):2 * P * (c % 2) + 2 * P],
                                  BK[half(g), 1, c, :], AR[half(g), c, :, :], start=True, stop=True)
                        if c:
                            last.then_inc(sig("rw_g2m"), 1)
                pe.wait_ge(sig("rw_g2"), 4 * i + 4)
                for g, c, hh in HH:
                    last = mm(ps[6][:, HD * hh:HD * hh + HD], G2[:, hh, 0:P], tokV[:, hh, :], start=True, stop=True)
                last.then_inc(sig("rw_avm"), 1)
                for n in range(len(LEVELS)):
                    for g in range(2):
                        if n == 0:
                            pe.wait_ge(sig("rw_t2"), i + 1)
                        else:
                            pe.wait_ge(sig("rw_te"), N_TE * i + level_steps(n - 1, g, 2))
                        for c in range(APAIRS):
                            last = mm(ps[g][:, P * c:P * c + P], G1[:, 3 * g + c, 0:P], Tm[:, 3 * g + c, :],
                                      start=True, stop=True)
                        last.then_inc(sig("rw_xm"), 1)
                    for g in range(2):
                        pe.wait_ge(sig("rw_x"), 2 * len(LEVELS) * i + 2 * n + g + 1)
                        if n < len(LEVELS) - 1:
                            for c in range(APAIRS):
                                last = mm(ps[2 + g][:, P * c:P * c + P], TT[:, 3 * g + c, :], X[:, 3 * g + c, :],
                                          start=True, stop=True)
                            last.then_inc(sig("rw_tm"), 1)
                        for c in range(APAIRS):
                            last = mm(ps[4 + g][:, P * c:P * c + P], X[:, 3 * g + c, :], TT[:, 3 * g + c, :],
                                      start=True, stop=True)
                        last.then_inc(sig("rw_tm"), 1)
                pe.wait_ge(sig("rw_rhs"), i + 1)
                for g in range(2):
                    pe.wait_ge(sig("rw_te"), N_TE * i + level_steps(len(LEVELS) - 1, g, 2))
                    for c in range(APAIRS):
                        last = mm(ps[g][:, P * c:P * c + P], TT[:, 3 * g + c, :], RHS[:, 3 * g + c, :],
                                  start=True, stop=True)
                    last.then_inc(sig("rw_wum"), 1)
                pe.wait_ge(sig("rw_wu"), 2 * i + 2)
                for g, c, hh in HH:
                    last = mm(ps[7][half(g), P * c:P * c + P], WU[:, hh, 0:HD], G1[:, hh, P:2 * P], start=True, stop=True)
                last.then_inc(sig("rw_gtm"), 1)
                for ch in range(2):
                    rows = half(ch)
                    for g, c, hh in HH:
                        mm(ps[2 + ch][half(g), HD * c:HD * c + HD], WU[rows, hh, 0:HD], tokBK[rows, 0, hh, :],
                           start=True, stop=True)
                    for g, c, hh in HH:
                        o = ps[2 + ch][half(g), HD * (APAIRS + c):HD * (APAIRS + c) + HD]
                        mm(o, tokBK[rows, 0, hh, :], WU[rows, hh, HD:P], start=True, stop=False)
                        last = mm(o, tokBK[rows, 1, hh, :], tokV[rows, hh, :], start=False, stop=True)
                    last.then_inc(sig("rw_pqm"), 1)
                for ch in range(2):
                    pe.wait_ge(sig("rw_pt"), 4 * i + 2 * ch + 2)
                    pe.wait_ge(sig("rw_state"), 3 * i + ch + 1)
                    for c in range(APAIRS):
                        last = mm(ps[4][:, HD * c:HD * c + HD], PT[:, ch, c, :], St[:, ch, c, :], start=True, stop=True)
                    last.then_inc(sig("rw_sm"), 1)
                    if ch == 0:
                        for g, c, hh in HH:
                            o = ps[5][half(g), P * c:P * c + P]
                            mm(o, WU[:, hh, HD:P], G1[:, hh, P:2 * P], start=True, stop=False)
                            last = mm(o, tokV[:, hh, :], G2[:, hh, P:2 * P], start=False, stop=True)
                        last.then_inc(sig("rw_yhm"), 1)
                pe.wait_ge(sig("rw_gt"), i + 1)
                pe.wait_ge(sig("rw_sbd"), 4 * i + 4)
                for ch in range(2):
                    for c in range(APAIRS):
                        last = mm(ps[6][:, P * c + HD * ch:P * c + HD * ch + HD], Sbd[:, ch, c, :],
                                  GT[:, c, HD * ch:HD * ch + HD], start=True, stop=True)
                last.then_inc(sig("rw_ygm"), 1)
            with pe.Fori(0, NT - 1) as i:
                rwkv_turn(i)
            rwkv_turn(NT - 1)

            def out_panel(j):
                tm_panel(pe, P_WO + j, (P_WO + j) % 2, [0, 1, 2, 3] if j < 4 else [4, 5, 6, 7], act_hi, act_lo, j % 4, 4,
                         T, last_first=True)

            def head_sums(bank, src, sem):
                mm(ps[bank][:, :], pair_ones[:, :], src, start=True, stop=True).then_inc(sig(sem), 1)
            pe.wait_ge(sig("rw_y"), NT + 1)
            for c in range(APAIRS):
                head_sums(4 + c, Y[:, c, :], "gn_sum")
            pe.wait_ge(sig("bonus_in"), 1)
            head_sums(7, yq[:, 0, 2, :], "bonus_sum")
            out_panel(0)
            for c in range(1, APAIRS):
                pe.wait_ge(sig("bonus_in"), c + 1)
                pe.wait_ge(sig("gn_mean"), c)
                head_sums(3 + c, yq[:, c, 2, :], "bonus_sum")
            for c in range(APAIRS):
                pe.wait_ge(sig("gn_sq"), c + 1)
                if c:
                    pe.wait_ge(sig("bonus_out"), c)
                head_sums((6, 7, 4)[c], yq[:, c, 0, :], "gn_var")
            out_panel(1)

            pe.wait_ge(sig("gn_eps"), APAIRS)
            keep_warm(7, 20)
            pe.wait_ge(sig("y_lo"), KT)
            for j in range(2, KT):
                out_panel(j)
            pe_memory(pe)
            pe_ffn(pe)

        @block.scalar
        def _(act_eng):
            act, A = act_eng, nc.scalar.activation
            gain_load(act, 0)
            pre_norm_act(act, 0, xt, junk[:, :], lambda t: (sig(f"x_loaded{t}"), 16), act_hi, [2, 3, 4, 5])
            gain_load(act, 1)
            act.wait_ge(*stage("pre_hn", 0, NT))
            gain_load(act, 2)
            for j in range(P_VB):
                act.wait_ge(sig("panel_used"), j + 1)
                if j < A_TILES:
                    if j >= 2:
                        act.wait_ge(sig("z_ready"), j - 1)
                    A(zraw[:, j % 2, 1:T + 1], ps[j % 2][:, :], ACT.Copy).then_inc(sig("w_in_out"), 1)
                else:
                    q = j - A_TILES
                    scale = -HD ** -0.5 if q < BW // P else HD ** -0.5 if 2 * BW // P <= q < (2 * BW + CW) // P else 1.0
                    A(qk[:, q, :], ps[j % 2][:, :], ACT.Copy, scale=scale).then_inc(sig("w_in_out"), 1)
            act.wait_ge(sig("z_ready"), A_TILES)
            A(z[0:LORA, A_TILES - 2, :], z[0:LORA, A_TILES - 2, :], ACT.Tanh).then_inc(sig("lora_in"), 1)
            A(z[:, A_TILES - 1, :], z[:, A_TILES - 1, :], ACT.Sigmoid).then_inc(sig("lora_in"), 1)
            act.wait_ge(sig("panel_used"), P_VC)
            for t in range(NT):
                A(vB[:, t, :], ps[4 + t][:, 0:VB_W], ACT.Copy).then_inc(sig("vB_out"), 1)
            for c in range(APAIRS):
                act.wait_ge(sig("lora_mm"), 3 * c + 1)
                A(sigw[:, c, :], ps[0][:, :], ACT.Sigmoid, bias=vecs[:, V_W0 + c:V_W0 + c + 1]).then_inc(sig("lora_out"), 1)
                act.wait_ge(sig("lora_mm"), 3 * c + 2)
                A(kka[:, c, :], ps[1][:, :], ACT.Sigmoid, bias=vecs[:, V_A0 + c:V_A0 + c + 1]).then_inc(sig("lora_out"), 1)
                act.wait_ge(sig("lora_mm"), 3 * c + 3)
                A(gate[:, c, :], ps[2][:, :], ACT.Copy).then_inc(sig("lora_out"), 1)
            for c in range(APAIRS):
                act.wait_ge(sig("kk_max"), c + 1)
                A(zs[:, c, :], zs[:, c, :], ACT.Ln).then_inc(sig("kk_ln"), 1)
            for c in range(APAIRS):
                act.wait_ge(sig("kk_ln"), c + 1)
                A(zs[:, c, :], zs[:, c, :], ACT.Exp, scale=-0.5).then_inc(sig("kk_norm"), 1)
            act.wait_ge(sig("lf_sum"), 1)
            A(lf2[:, :, :], lf[:, :, :], ACT.Abs).then_inc(sig("lf_exp"), 1)
            act.wait_ge(sig("lf_exp"), 1)
            A(lf2[:, :, :], lf2[:, :, :], ACT.Exp, scale=-1.0).then_inc(sig("lf_exp"), 1)
            act.wait_ge(sig("lf_exp"), 2)
            A(lf2[:, :, :], lf2[:, :, :], ACT.Ln, bias=1.0).then_inc(sig("lf_exp"), 1)
            act.wait_ge(sig("panel_used"), P_WO)
            for t in range(NT):
                A(vC[:, t, :], ps[4 + t][:, 0:VC_W], ACT.Copy).then_inc(sig("vC_out"), 1)

            def y_high(n, src, bank_ready):
                act.wait_ge(*bank_ready)
                A(act_hi[:, n, :], src, ACT.Copy).then_inc(sig("y_hi"), 1)

            def fox_exp(n):
                h, i = FOX[n]
                w = P * (i + 1)
                act.wait_ge(sig("fox_min"), n + 1)
                if n >= 3:
                    act.wait_ge(sig("fox_tr"), n - 2)
                A(fp[:, n % 3, 0:w], fs[:, n % 3, 0:w], ACT.Exp, bias=small_t[:, n % 4, 0:1], scale=-1.0,
                  accum_out=small_t[:, n % 4, 1:2]).then_inc(sig("fox_exp"), 1)

            def fox_pt(n):
                h, i = FOX[n]
                w = P * (i + 1)
                act.wait_ge(sig("fox_tr"), n + 1)
                if n >= 2:
                    act.wait_ge(sig("fox_pv"), n - 1)
                A(fpt[:, n % 2, 0:w], ps[4 + n % 2][:, 0:w], ACT.Copy).then_inc(sig("fox_pt"), 1)

            def stick_soft_exp(h):
                act.wait_ge(sig("stick_over"), NT * h + NT)
                A(se[:, :], se[:, :], ACT.Exp).then_inc(sig("stick_log"), 1)

            def stick_soft_ln(h):
                act.wait_ge(sig("stick_log"), 2 * h + 1)
                A(se[:, :], se[:, :], ACT.Ln, bias=1.0).then_inc(sig("stick_log"), 1)

            def stick_exp(n):
                h, j = STK[n]
                act.wait_ge(sig("stick_cum"), n + 1)
                if n == 0:
                    act.wait_ge(sig("fox_min"), len(FOX))
                    act.wait_ge(sig("fox_pv"), len(FOX))
                if h >= 2:
                    act.wait_ge(sig("stick_pv"), h - 1)
                A(satt[:, h % 2, OJ[j]:OJ[j] + NJ[j]], ps[4 + n % 2][:, 0:NJ[j]], ACT.Exp).then_inc(sig("stick_exp"), 1)

            for n in range(len(FOX) + 3):
                if n < len(FOX):
                    h, i = FOX[n]
                    if i == 0:
                        act.wait_ge(sig("cb_mm"), h + 1)
                        if h >= 2:
                            act.wait_ge(sig("fox_min"), NT * (h - 1))
                        A(cb[:, h % 2, :], ps[7][:, :], ACT.Copy).then_inc(sig("cb_out"), 1)
                    fox_exp(n)
                if 2 <= n < len(FOX) + 2:
                    fox_pt(n - 2)
                if n == len(FOX):
                    stick_soft_exp(0)
                if n == len(FOX) + 1:
                    stick_soft_ln(0)
                if n >= 3 and (n - 3) % (2 * NT) == 2 * NT - 1:
                    c = (n - 3) // (2 * NT)
                    y_high(APAIRS + c, ps[6][:, :], (sig("fox_pv"), 2 * NT * (c + 1)))
            for h in range(CH):
                stick_exp(NT * h)
                stick_exp(NT * h + 1)
                if h + 1 < CH:
                    stick_soft_exp(h + 1)
                    stick_soft_ln(h + 1)
                stick_exp(NT * h + 2)
                stick_exp(NT * h + 3)
                if h == 2:
                    y_high(2 * APAIRS, ps[6][:, :], (sig("stick_pv"), 2))
            y_high(2 * APAIRS + 1, ps[7][:, :], (sig("stick_pv"), 4))

            def rwkv_decays(i):
                now = bass.ds(P * i, P)
                if type(i) is not int:
                    act.wait_ge(sig("rw_in"), i)
                A(E[:, 0], clog[:, :, now], ACT.Exp, scale=-DECAY_C).then_inc(sig("rw_E"), 1)
                A(E[:, 1], clog[:, :, now], ACT.Exp, scale=DECAY_C).then_inc(sig("rw_E"), 1)
                A(E[:, 2], sigw[:, :, now], ACT.Exp, scale=-DECAY_C).then_inc(sig("rw_E"), 1)
                A(Vt[:, :, :], z[:, 2 * APAIRS:3 * APAIRS, now], ACT.Copy).then_inc(sig("rw_vt"), 1)

            def rwkv_act(i, more):
                now = bass.ds(P * i, P)
                for kind in range(4):
                    act.wait_ge(sig("rw_tr"), 4 * i + kind + 1)
                    to = (RHS[:, :, 0:HD], tokBK[:, 0], tokBK[:, 1], tokV[:, :, :])[kind]
                    A(to.rearrange("p (g c) d -> p c g d", g=2),
                      ps[kind][:, 0:AW].rearrange("p (c g d) -> p c g d", c=APAIRS, g=2), ACT.Copy).then_inc(sig("rw_tok"), 1)
                act.wait_ge(sig("rw_avm"), i + 1)
                A(RHS[:, :, HD:P], ps[6][:, 0:AW].rearrange("p (h d) -> p h d", h=AH), ACT.Copy).then_inc(sig("rw_rhs"), 1)
                if more:
                    rwkv_decays(i + 1)
                three = "p (c n) -> p c n"
                for n in range(len(LEVELS)):
                    for g in range(2):
                        for which in ((1, 2) if n < len(LEVELS) - 1 else (2,)):
                            act.wait_ge(sig("rw_tm"), N_TE * i + level_steps(n, g, which))
                            A((Tm if which == 1 else TT)[:, 3 * g:3 * g + 3, :],
                              ps[2 * which + g][:, 0:AW].rearrange(three, c=3), ACT.Copy).then_inc(sig("rw_te"), 1)
                for g in range(2):
                    act.wait_ge(sig("rw_wum"), 2 * i + g + 1)
                    A(WU[:, 3 * g:3 * g + 3, :], ps[g][:, 0:AW].rearrange(three, c=3), ACT.Copy).then_inc(sig("rw_wu"), 1)
                for ch in range(2):
                    act.wait_ge(sig("rw_pqm"), 2 * i + ch + 1)
                    A(QS[:, ch], ps[2 + ch][:, AW // 2:AW].rearrange(three, c=3), ACT.Copy).then_inc(sig("rw_q"), 1)
                act.wait_ge(sig("rw_yhm"), i + 1)
                A(Y[:, :, now], ps[5][:, 0:AW].rearrange(three, c=3), ACT.Copy).then_inc(sig("rw_yh"), 1)
                for ch in range(2):
                    act.wait_ge(sig("rw_state"), 3 * i + ch + 1)
                    for g in range(2):
                        A(Sbd[half(g), ch, :, HD * g:HD * g + HD], St[half(g), ch], ACT.Copy).then_inc(sig("rw_sbd"), 1)

            act.wait_ge(sig("stick_pv"), CH)
            rwkv_decays(0)
            act.wait_ge(sig("rw_zero"), 3)
            with act.Fori(0, NT - 1) as i:
                rwkv_act(i, True)
            rwkv_act(NT - 1, False)

            for c in range(APAIRS):
                act.wait_ge(sig("gn_eps"), c + 1)
                A(yq[:, c, 0, :], yq[:, c, 0, :], ACT.Ln).then_inc(sig("gn_ln"), 1)
            for c in range(APAIRS):
                act.wait_ge(sig("gn_ln"), c + 1)
                A(yq[:, c, 1, :], yq[:, c, 0, :], ACT.Exp, scale=-0.5).then_inc(sig("gn_std"), 1)
            for c in range(APAIRS):
                y_high(c, Y[:, c, :], (sig("y_a"), c + 1))
            act_memory(act, A)
            act_ffn(act, A)

        @block.vector
        def _(dve):
            V = nc.vector
            own = Steps(dve, sig("dve_steps"))
            step, sync = own.step, own.sync
            pre_norm_dve(dve, 0, xt, hn, 0, act_hi, act_lo, [2, 3, 4, 5], lambda t: None)
            dve.wait_ge(sig("vecs_ps"), 1)
            V.tensor_copy(vecs[:, :], ps[7][:, 0:V_ROWS]).then_inc(sig("vecs_ready"), 1)
            dve.wait_ge(sig("vecs_ready"), 1)
            for j in range(A_TILES):
                dve.wait_ge(sig("w_in_out"), j + 1)
                now, before = zraw[:, j % 2, 1:T + 1], zraw[:, j % 2, 0:T]
                step(V.tensor_tensor(z[:, j, :], before, now, ALU.subtract))
                sync()
                V.scalar_tensor_tensor(z[:, j, :], z[:, j, :], vecs[:, V_MU + j:V_MU + j + 1], now, ALU.mult, ALU.add)\
                    .then_inc(sig("z_ready"), 1)
            dve.wait_ge(sig("z_ready"), A_TILES)
            step(V.tensor_scalar(omka[:, :], vecs[:, V_KA:V_KA + APAIRS], -1.0, 1.0, ALU.mult, ALU.add))
            for c in range(APAIRS):
                step(V.tensor_scalar(nkk[:, c, :], z[:, APAIRS + c, :], vecs[:, V_KK + c:V_KK + c + 1], None, ALU.mult))
            sync()
            for c in range(APAIRS):
                V.tensor_tensor(clog[:, c, :], nkk[:, c, :], nkk[:, c, :], ALU.mult).then_inc(sig("kk_squared"), 1)
            dve.wait_ge(sig("vB_out"), NT)
            dve.wait_ge(sig("small_loaded"), SMALL_LOADS)
            V.tensor_tensor(lf[:, :, :], vB[:, :, BW:VB_W], fbias[:, :].unsqueeze(1).to_broadcast([P, NT, BH]), ALU.add)\
                .then_inc(sig("lf_sum"), 1)
            for c in range(APAIRS):
                dve.wait_ge(sig("kk_sums"), c + 1)
                V.tensor_scalar(zs[:, c, :], ps[3][:, :], 1e-24, None, ALU.max).then_inc(sig("kk_max"), 1)
            dve.wait_ge(sig("lora_out"), 3 * APAIRS)
            for c in range(APAIRS):
                step(V.tensor_scalar(hn[:, c // 2, T * (c % 2):T * (c % 2) + T], kka[:, c, :], vecs[:, V_KA + c:V_KA + c + 1], omka[:, c:c + 1],
                                     ALU.mult, ALU.add))
            sync()
            for c in range(APAIRS):
                step(V.tensor_tensor(z[:, APAIRS + c, :], z[:, APAIRS + c, :], hn[:, c // 2, T * (c % 2):T * (c % 2) + T], ALU.mult))
            for c in range(APAIRS):
                dve.wait_ge(sig("kk_norm"), c + 1)
                step(V.scalar_tensor_tensor(nkk[:, c, :], nkk[:, c, :], -1.0, zs[:, c, :], ALU.mult, ALU.mult))
            sync()
            for c in range(APAIRS):
                step(V.scalar_tensor_tensor(kka[:, c, :], nkk[:, c, :], -1.0, kka[:, c, :], ALU.mult, ALU.mult))
            dve.wait_ge(sig("lf_exp"), 3)
            V.scalar_tensor_tensor(lf[:, :, :], lf[:, :, :], 0.0, lf2[:, :, :], ALU.min, ALU.subtract)\
                .then_inc(sig("lf_ready"), 1)
            dve.wait_ge(sig("constants_ready"), 1)
            for c in range(APAIRS):
                step(V.tensor_tensor_scan(clog[:, c, :], reset[:, :], sigw[:, c, :], 0.0, ALU.mult, ALU.add))
            sync()
            for c in range(APAIRS):
                step(V.tensor_tensor(sigw[:, c, :], clog[:, c, :], sigw[:, c, :], ALU.subtract))

            def y_low(n, src):
                dve.wait_ge(sig("y_hi"), (n - APAIRS if n >= APAIRS else n + KT - APAIRS) + 1)
                V.tensor_tensor(act_lo[:, n, :], src, act_hi[:, n, :].bitcast(F32), ALU.subtract).then_inc(sig("y_lo"), 1)

            def fox_min(n):
                h, i = FOX[n]
                w = P * (i + 1)
                dve.wait_ge(sig("fox_mm"), n + 1)
                dve.wait_ge(sig("cb_out"), h + 1)
                if n >= 3:
                    dve.wait_ge(sig("fox_exp"), n - 2)
                V.tensor_tensor_reduce(out=fs[:, n % 3, 0:w], in0=ps[row_bank(n)][:, 0:w], in1=cb[:, h % 2, 0:w],
                                       scale=1.0, scalar=3.0e38, op0=ALU.add, op1=ALU.min,
                                       accum_out=small_t[:, n % 4, 0:1]).then_inc(sig("fox_min"), 1)

            def fox_norm(n):
                h, i = FOX[n]
                w = P * (i + 1)
                dve.wait_ge(sig("fox_exp"), n + 1)
                V.reciprocal(small_t[:, n % 4, 2:3], small_t[:, n % 4, 1:2]).then_inc(sig("fox_recip"), 1)
                dve.wait_ge(sig("fox_recip"), n + 1)
                V.tensor_scalar(fp[:, n % 3, 0:w], fp[:, n % 3, 0:w], small_t[:, n % 4, 2:3], None, ALU.mult)\
                    .then_inc(sig("fox_norm"), 1)

            def stick_clip(n):
                h, j = STK[n]
                cols = slice(OJ[j], OJ[j] + NJ[j])
                dve.wait_ge(sig("stick_mm"), n + 1)
                if h >= 2 and n % NT == 0:
                    dve.wait_ge(sig("stick_cum"), NT * (h - 1))
                V.tensor_scalar(se[:, cols], ps[row_bank(n)][:, 0:NJ[j]], CLIP, None, ALU.min)
                V.tensor_scalar(sp[h % 2][:, cols], ps[row_bank(n)][:, 0:NJ[j]], CLIP, -CLIP, ALU.max, ALU.add)\
                    .then_inc(sig("stick_over"), 1)

            def stick_sp(h):
                dve.wait_ge(sig("stick_over"), NT * h + NT)
                dve.wait_ge(sig("stick_log"), 2 * h + 2)
                V.tensor_tensor(sp[h % 2], sp[h % 2], se[:, :], ALU.add).then_inc(sig("stick_sum"), 1)
                dve.wait_ge(sig("stick_sum"), h + 1)
                for j in range(NT):
                    to = sp[h % 2][:, OJ[j]:OJ[j] + P]
                    last = V.tensor_tensor(to, to, smask[:, :], ALU.mult)
                last.then_inc(sig("stick_sp"), 1)

            for n in range(len(FOX) + 3):
                if n < len(FOX):
                    fox_min(n)
                if 1 <= n < len(FOX) + 1:
                    fox_norm(n - 1)
                if n == len(FOX) - 3:
                    stick_clip(0)
                    stick_clip(1)
                if n == len(FOX) - 1:
                    stick_clip(2)
                    stick_clip(3)
                if n >= 3 and (n - 3) % (2 * NT) == 2 * NT - 1:
                    y_low(APAIRS + (n - 3) // (2 * NT), ps[6][:, :])
            for h in range(CH):
                stick_sp(h)
                if h + 1 < CH:
                    for e in range(NT):
                        stick_clip(NT * (h + 1) + e)
                if h == 3:
                    y_low(2 * APAIRS, ps[6][:, :])
            y_low(2 * APAIRS + 1, ps[7][:, :])

            def pre_bk(i):
                pre, now = Steps(dve, sig("rw_pre"), RW_PRE * i), bass.ds(P * i, P)
                dve.wait_ge(sig("rw_E"), 3 * i + 2)
                pre.step(V.tensor_tensor(BK[:, 0], kka[:, :, now], E[:, 1], ALU.mult))
                pre.step(V.tensor_tensor(BK[:, 1], z[:, APAIRS:2 * APAIRS, now], E[:, 1], ALU.mult))

            chunk_ends = E[:, 0].rearrange("p c (b j) -> p b c j", b=2)[:, :, :, CHUNK - 1:CHUNK]

            def pre_r(i):
                pre, now = Steps(dve, sig("rw_pre"), RW_PRE * i + 2), bass.ds(P * i, P)
                pre.step(V.tensor_tensor(AR[:, :, 1, :], z[:, 0:APAIRS, now], E[:, 0], ALU.mult))
                pre.step(V.tensor_copy(ends[:, :, :, :], chunk_ends))

            def pre_bkh(i):
                pre = Steps(dve, sig("rw_pre"), RW_PRE * i + 4)
                pre.sync()
                for n in range(2):
                    pre.step(V.tensor_tensor(BKh[:, n].rearrange("p c (b j) -> p b c j", b=2),
                                             BK[:, n].rearrange("p c (b j) -> p b c j", b=2),
                                             ends[:, :, :, :].to_broadcast([P, 2, APAIRS, CHUNK]), ALU.mult))

            def pre_a(i):
                Steps(dve, sig("rw_pre"), RW_PRE * i + 6).sync()
                dve.wait_ge(sig("rw_E"), 3 * i + 3)
                V.tensor_tensor(AR[:, :, 0, :], nkk[:, :, bass.ds(P * i, P)], E[:, 2], ALU.mult).then_inc(sig("rw_in"), 1)

            PRE = (pre_bk, pre_r, pre_bkh, pre_a)

            def rwkv_dve(i, more):
                now = bass.ds(P * i, P)
                turn = Steps(dve, sig("rw_dve"), RW_STEPS * i)
                V.tensor_copy(St[:, 0], St[:, 2]).then_inc(sig("rw_state"), 1)
                dve.wait_ge(sig("rw_in"), i + 1)

                def masked(to, bank, heads, sem):
                    V.tensor_tensor(to, ps[bank][:, 0:2 * P * heads].rearrange("p (h n) -> p h n", h=heads),
                                    grams[:, :].unsqueeze(1).to_broadcast([P, heads, 2 * P]), ALU.mult).then_inc(sem, 1)
                for g in range(2):
                    for b in range(2):
                        dve.wait_ge(sig("rw_g1m"), 4 * i + 2 * g + b + 1)
                        masked(G1[:, 3 * g + 2 * b:3 * g + 2 + b, :], 4 + 2 * g + b, 2 - b, sig("rw_g1"))
                dve.wait_ge(sig("rw_g1"), 4 * i + 4)
                eye = ident[:, :].unsqueeze(1).to_broadcast([P, AH, P])
                turn.step(V.tensor_tensor(G1[:, :, 0:P], G1[:, :, 0:P], eye, ALU.add))

                def masked2(g, b):
                    dve.wait_ge(sig("rw_g2m"), 4 * i + 2 * g + b + 1)
                    masked(G2[:, 3 * g + 2 * b:3 * g + 2 + b, :], 2 * g + b, 2 - b, sig("rw_g2"))
                masked2(0, 0)
                for g in range(2):
                    dve.wait_ge(sig("rw_nm"), 2 * i + g + 1)
                    turn.step(V.tensor_tensor(Tm[:, 3 * g:3 * g + 3, :], ps[4 + 2 * g][:, 0:AW].rearrange("p (h n) -> p h n", h=3),
                                              lowm[:, :].unsqueeze(1).to_broadcast([P, 3, P]), ALU.mult))
                masked2(0, 1)
                masked2(1, 0)
                masked2(1, 1)
                turn.sync()
                turn.step(V.tensor_tensor(Tm[:, :, :], Tm[:, :, :], eye, ALU.add))
                V.tensor_tensor(TT[:, :, :], G1[:, :, 0:P], lowmT[:, :].unsqueeze(1).to_broadcast([P, AH, P]), ALU.mult)\
                    .then_inc(sig("rw_t2"), 1)
                turn.step(V.tensor_copy(Rs[:, :, :], AR[:, :, 1, :]))
                for ch in range(2):
                    turn.step(V.tensor_tensor(Dg[:, ch], stack_id[:, :].unsqueeze(1).to_broadcast([P, APAIRS, HD]),
                                              ends[:, ch].to_broadcast([P, APAIRS, HD]), ALU.mult))
                for n in range(len(LEVELS)):
                    for g in range(2):
                        dve.wait_ge(sig("rw_xm"), 2 * len(LEVELS) * i + 2 * n + g + 1)
                        V.tensor_tensor(X[:, 3 * g:3 * g + 3, :], ps[g][:, 0:AW].rearrange("p (h n) -> p h n", h=3),
                                        levm[:, n, :].unsqueeze(1).to_broadcast([P, 3, P]), ALU.mult).then_inc(sig("rw_x"), 1)
                    if more and n < len(PRE):
                        PRE[n](i + 1)
                turn.sync()
                for ch in range(2):
                    dve.wait_ge(sig("rw_q"), 2 * i + ch + 1)
                    for g in range(2):
                        V.tensor_tensor(PT[half(g), ch, :, HD * g:HD * g + HD],
                                        ps[2 + ch][half(g), 0:AW // 2].rearrange("p (c n) -> p c n", c=3),
                                        Dg[half(g), ch], ALU.add).then_inc(sig("rw_pt"), 1)
                dve.wait_ge(sig("rw_gtm"), i + 1)
                V.tensor_tensor(GT[:, :, :], ps[7][:, 0:AW].rearrange("p (c n) -> p c n", c=3), Rs[:, :, :], ALU.add)\
                    .then_inc(sig("rw_gt"), 1)
                for ch in range(2):
                    dve.wait_ge(sig("rw_sm"), 2 * i + ch + 1)
                    V.tensor_tensor(St[:, ch + 1], ps[4][:, 0:AW // 2].rearrange("p (c n) -> p c n", c=3), QS[:, ch], ALU.add)\
                        .then_inc(sig("rw_state"), 1)
                dve.wait_ge(sig("rw_ygm"), i + 1)
                dve.wait_ge(sig("rw_yh"), i + 1)
                dve.wait_ge(sig("rw_state"), 3 * i + 3)
                V.tensor_tensor(Y[:, :, now], ps[6][:, 0:AW].rearrange("p (c n) -> p c n", c=3), Y[:, :, now], ALU.add)\
                    .then_inc(sig("rw_y"), 1)

            sync()
            dve.wait_ge(sig("y_lo"), APAIRS + CH // 2)
            for part in PRE:
                part(0)
            V.memset(PT[:, :, :, :], 0.0).then_inc(sig("rw_zero"), 1)
            V.memset(Sbd[:, :, :, :], 0.0).then_inc(sig("rw_zero"), 1)
            V.memset(St[:, 2], 0.0).then_inc(sig("rw_zero"), 1)
            dve.wait_ge(sig("rw_zero"), 3)
            V.nop().then_inc(sig("rw_y"), 1)
            with dve.Fori(0, NT - 1) as i:
                rwkv_dve(i, True)
            rwkv_dve(NT - 1, False)
            fin = Steps(dve, sig("fin_steps"))
            dve.wait_ge(sig("rw_y"), NT + 1)
            for c in range(APAIRS):
                V.scalar_tensor_tensor(yq[:, c, 2, :], z[:, c, :], vecs[:, V_RK + c:V_RK + c + 1], z[:, APAIRS + c, :],
                                       ALU.mult, ALU.mult).then_inc(sig("bonus_in"), 1)
            for c in range(APAIRS):
                dve.wait_ge(sig("gn_sum"), c + 1)
                V.scalar_tensor_tensor(Y[:, c, :], ps[4 + c][:, :], -1.0 / HD, Y[:, c, :], ALU.mult, ALU.add)\
                    .then_inc(sig("gn_mean"), 1)
            dve.wait_ge(sig("gn_mean"), APAIRS)
            for c in range(APAIRS):
                V.tensor_tensor(yq[:, c, 0, :], Y[:, c, :], Y[:, c, :], ALU.mult).then_inc(sig("gn_sq"), 1)
            for c in range(APAIRS):
                dve.wait_ge(sig("bonus_sum"), c + 1)
                V.tensor_tensor(yq[:, c, 3, :], ps[(7, 4, 5)[c]][:, :], z[:, 2 * APAIRS + c, :], ALU.mult)\
                    .then_inc(sig("bonus_out"), 1)
            for c in range(APAIRS):
                dve.wait_ge(sig("gn_var"), c + 1)
                V.tensor_scalar(yq[:, c, 0, :], ps[(6, 7, 4)[c]][:, :], 1.0 / HD, GN_EPS, ALU.mult, ALU.add).then_inc(sig("gn_eps"), 1)
            dve.wait_ge(sig("bonus_out"), APAIRS)
            for c in range(APAIRS):
                fin.step(V.tensor_scalar(yq[:, c, 3, :], yq[:, c, 3, :], vecs[:, V_GB + c:V_GB + c + 1], None, ALU.add))
            for c in range(APAIRS):
                dve.wait_ge(sig("gn_std"), c + 1)
                fin.step(V.scalar_tensor_tensor(Y[:, c, :], Y[:, c, :], vecs[:, V_GG + c:V_GG + c + 1], yq[:, c, 1, :],
                                                ALU.mult, ALU.mult))
            for c in range(APAIRS):
                fin.sync(APAIRS + c + 1)
                fin.step(V.tensor_tensor(Y[:, c, :], Y[:, c, :], yq[:, c, 3, :], ALU.add))
            for c in range(APAIRS):
                fin.sync(2 * APAIRS + c + 1)
                V.tensor_tensor(Y[:, c, :], Y[:, c, :], gate[:, c, :], ALU.mult).then_inc(sig("y_a"), 1)
            for c in range(APAIRS):
                y_low(c, Y[:, c, :])
            dve_memory(dve, V)
            dve_ffn(dve, V)


_INS = ["x", "mem", "norm_mix_pre", "norm_mix_post", "w_in", "shift_mu", "rwkv_w0", "rwkv_w_up", "rwkv_a0", "rwkv_a_up",
        "rwkv_g_up", "rwkv_k_k", "rwkv_k_a", "rwkv_r_k", "rwkv_gn_g", "rwkv_gn_b", "fox_f_bias", "w_out", "norm_mem_pre",
        "norm_mem_post", "norm_mem_kv", "mem_wq", "mem_wkv", "mem_wo", "norm_ffn_pre", "norm_ffn_post", "ffn_w_gu",
        "ffn_w_down"]


def kernel(**inputs):
    import numpy as _np
    import concourse.bacc as _bacc
    from concourse import mybir as _mybir
    from concourse.bass_utils import run_bass_kernel_spmd as _run

    nc = _bacc.Bacc("TRN2", target_bir_lowering=False, num_devices=1)
    arrays, args = {}, []
    for name in _INS:
        a = _np.ascontiguousarray(inputs[name])
        arrays[f"in_{name}"] = a
        args.append(nc.dram_tensor(f"in_{name}", a.shape, _mybir.dt.from_np(a.dtype), kind="ExternalInput").ap())
    args.append(nc.dram_tensor("out_0", (1, T, D), F32, kind="ExternalOutput").ap())
    hybrid_block(nc, *args)
    r = _run(nc, [arrays], core_ids=[0])
    return r.results[0]["out_0"]
```
